# Optimizing a Trainium2 kernel written in Bass

```python
import functools
import jax, jax.numpy as jnp
from jax import lax
import numpy as np

D_MODEL = 1024
BATCH = 1
SEQ = 512
DEPTH = 1
DEC_BATCH = 8
DEC_SEQ = 1
PAST_LEN = 2048
PAGE_SIZE = 128

BRANCH_W = 512
HA = 8
DA = BRANCH_W // HA
WA = HA * DA
WB = BRANCH_W
NBLK_B = 8
BB = WB // NBLK_B
CONV_B = 4
LRU_C = 8.0
WC = BRANCH_W
CONV_C = 31
N_BRANCH = 3
D_IN = 3 * WA + 2 * WB + 2 * WC + N_BRANCH * D_MODEL
N_EXPERTS = 32
TOP_K = 4
D_FF = D_MODEL
SWIGLU_LIMIT = 7.0
SWIGLU_ALPHA = 1.702
Q_BLOCK = 128
DN_ALPHA = (2 * DEPTH) ** 0.25
DN_BETA = (8 * DEPTH) ** -0.25
LN_EPS = 1e-5
SB_BIAS_HI = -5.0
SB_BIAS_LO = -9.0

kernel_name = "hybrid_sb_rglru_conformer_moe_step"

def layer_norm(x, g, b):
    xf = x.astype(jnp.float32)
    mu = jnp.mean(xf, axis=-1, keepdims=True)
    var = jnp.mean(jnp.square(xf - mu), axis=-1, keepdims=True)
    return ((xf - mu) * lax.rsqrt(var + LN_EPS)).astype(x.dtype) * g + b

def sb_block(q, k, v, bias, q_pos, k_pos):
    z = jnp.einsum("bqhd,bkhd->bhqk", q, k).astype(jnp.float32) * (DA ** -0.5) \
        + bias.astype(jnp.float32)[None, :, None, None]
    causal = k_pos[None, :] < q_pos[:, None]
    log_rest = jnp.where(causal, jax.nn.log_sigmoid(-z), 0.0)
    after = lax.cumsum(log_rest, axis=3, reverse=True) - log_rest
    w = jnp.where(causal, jnp.exp(jax.nn.log_sigmoid(z) + after), 0.0)
    return jnp.einsum("bhqk,bkhd->bqhd", w.astype(v.dtype), v)

def sb_prompt(q, k, v, bias):
    b, s = q.shape[0], q.shape[1]
    nb = s // Q_BLOCK
    qb = q.reshape(b, nb, Q_BLOCK, HA, DA).transpose(1, 0, 2, 3, 4)
    k_pos = jnp.arange(s)

    def one_block(args):
        i, qi = args
        q_pos = i * Q_BLOCK + jnp.arange(Q_BLOCK)
        return sb_block(qi, k, v, bias, q_pos, k_pos)

    o = lax.map(one_block, (jnp.arange(nb), qb))
    return o.transpose(1, 0, 2, 3, 4).reshape(b, s, HA, DA)

def sb_sample(q, k, v, bias, k_past, v_past):
    past = k_past.shape[1]
    t = q.shape[1]
    k_all = jnp.concatenate([k_past.astype(k.dtype), k], axis=1)
    v_all = jnp.concatenate([v_past.astype(v.dtype), v], axis=1)
    return sb_block(q, k_all, v_all, bias, past + jnp.arange(t), jnp.arange(past + t))

def gather_pages(pool, page_table):
    g = pool[page_table]
    return g.reshape(g.shape[0], g.shape[1] * g.shape[2], g.shape[3], g.shape[4])

def causal_depthwise_conv(x, buf, w, b):
    xp = jnp.concatenate([buf.astype(x.dtype), x], axis=1)
    y = lax.conv_general_dilated(xp, w[:, None, :].astype(x.dtype), window_strides=(1,), padding="VALID",
                                 dimension_numbers=("NWC", "WIO", "NWC"), feature_group_count=x.shape[-1])
    return y + b, xp[:, xp.shape[1] - (w.shape[0] - 1):]

def rg_lru(x, h0, wa, ba, wx, bx, lam):
    b, t, _ = x.shape
    xb = x.reshape(b, t, NBLK_B, BB)
    r = jax.nn.sigmoid(jnp.einsum("btni,nij->btnj", xb, wa).reshape(b, t, WB) + ba)
    i = jax.nn.sigmoid(jnp.einsum("btni,nij->btnj", xb, wx).reshape(b, t, WB) + bx)
    log_a = LRU_C * r.astype(jnp.float32) * jax.nn.log_sigmoid(lam.astype(jnp.float32))
    a = jnp.exp(log_a)
    u = jnp.sqrt(-jnp.expm1(2.0 * log_a)) * (i * x).astype(jnp.float32)

    def step(h, au):
        a_t, u_t = au
        h = a_t * h + u_t
        return h, h

    h_last, hs = lax.scan(step, h0.astype(jnp.float32), (a.transpose(1, 0, 2), u.transpose(1, 0, 2)))
    return hs.transpose(1, 0, 2).astype(x.dtype), h_last.astype(x.dtype)

def moe_block_size(n_assign):
    blk = 128
    while blk > 8 and blk * N_EXPERTS > n_assign:
        blk //= 2
    return blk

def moe(x, router_w, router_b, w_gate, b_gate, w_up, b_up, w_down, b_down):
    b, t, d = x.shape
    xt = x.reshape(b * t, d)
    n_tok = xt.shape[0]
    logits = (xt @ router_w + router_b).astype(jnp.float32)
    top_val, top_idx = lax.top_k(logits, TOP_K)
    gate_w = jax.nn.softmax(top_val, axis=-1).astype(x.dtype)
    n_assign = n_tok * TOP_K
    blk = moe_block_size(n_assign)
    flat_e = top_idx.reshape(-1)
    order = jnp.argsort(flat_e)
    sorted_e = flat_e[order]
    sorted_tok = (order // TOP_K).astype(jnp.int32)
    counts = jnp.bincount(flat_e, length=N_EXPERTS)
    padded = (counts + blk - 1) // blk * blk
    starts = jnp.cumsum(counts) - counts
    ends_p = jnp.cumsum(padded)
    pstarts = ends_p - padded
    dest = pstarts[sorted_e] + (jnp.arange(n_assign) - starts[sorted_e])
    n_blocks = -(-n_assign // blk) + N_EXPERTS
    tok_buf = jnp.full((n_blocks * blk,), n_tok, jnp.int32).at[dest].set(sorted_tok)
    block_e = jnp.clip(jnp.searchsorted(ends_p, jnp.arange(n_blocks) * blk, side="right"), 0, N_EXPERTS - 1)
    x_pad = jnp.concatenate([xt, jnp.zeros((1, d), xt.dtype)], axis=0)
    xb = x_pad[tok_buf].reshape(n_blocks, blk, d)

    def expert_block(args):
        xi, e = args
        g = jnp.minimum(xi @ w_gate[e] + b_gate[e], SWIGLU_LIMIT)
        u = jnp.clip(xi @ w_up[e] + b_up[e], -SWIGLU_LIMIT, SWIGLU_LIMIT)
        h = (u + 1.0) * (g * jax.nn.sigmoid(SWIGLU_ALPHA * g))
        return h @ w_down[e] + b_down[e]

    yb = lax.map(expert_block, (xb, block_e)).reshape(n_blocks * blk, d)
    y_sorted = yb[dest]
    y_assign = jnp.zeros_like(y_sorted).at[order].set(y_sorted).reshape(n_tok, TOP_K, d)
    return jnp.einsum("tk,tkd->td", gate_w, y_assign).reshape(b, t, d)

def trunk_layer(x, attend, h0, lru_buf0, conf_buf0,
                w_in, b_merge, sb_bias, lru_conv_w, lru_conv_b, lru_wa, lru_ba, lru_wx, lru_bx, lru_lambda,
                conf_conv_w, conf_conv_b, conf_ln_g, conf_ln_b, w_branch, w_out, ln1_g, ln1_b,
                router_w, router_b, w_gate, b_gate, w_up, b_up, w_down, b_down, ln2_g, ln2_b):
    b, t, _ = x.shape
    proj = x @ w_in
    splits = [WA, 2 * WA, 3 * WA, 3 * WA + WB, 3 * WA + 2 * WB, 3 * WA + 2 * WB + WC, 3 * WA + 2 * WB + 2 * WC]
    q, k, v, lru_x, lru_g, glu_a, glu_b, gates = jnp.split(proj, splits, axis=-1)
    q = q.reshape(b, t, HA, DA)
    k = k.reshape(b, t, HA, DA)
    v = v.reshape(b, t, HA, DA)
    o_a = attend(q, k, v, sb_bias).reshape(b, t, WA)
    xc, lru_buf = causal_depthwise_conv(lru_x, lru_buf0, lru_conv_w, lru_conv_b)
    hs, h_last = rg_lru(xc, h0, lru_wa, lru_ba, lru_wx, lru_bx, lru_lambda)
    o_b = hs * jax.nn.gelu(lru_g)
    glu = glu_a * jax.nn.sigmoid(glu_b)
    cc, conf_buf = causal_depthwise_conv(glu, conf_buf0, conf_conv_w, conf_conv_b)
    o_c = jax.nn.silu(layer_norm(cc, conf_ln_g, conf_ln_b))
    branches = jnp.stack([o_a, o_b, o_c], axis=2)
    bproj = jnp.einsum("btnw,nwd->btnd", branches, w_branch)
    g = jax.nn.sigmoid(gates.reshape(b, t, N_BRANCH, D_MODEL) + b_merge)
    merged = jnp.sum(g * bproj, axis=2)
    x = layer_norm(DN_ALPHA * x + merged @ w_out, ln1_g, ln1_b)
    x = layer_norm(DN_ALPHA * x + moe(x, router_w, router_b, w_gate, b_gate, w_up, b_up, w_down, b_down), ln2_g, ln2_b)
    return x, k, v, h_last, lru_buf, conf_buf

def _normal(key, shape, scale):
    return jax.random.normal(key, shape, jnp.float32) * scale

def setup_inputs(seed: int = 0) -> dict:
    key = jax.random.key(seed)
    ks = jax.random.split(key, 40)
    n_pages = PAST_LEN // PAGE_SIZE
    n_used = DEC_BATCH * n_pages
    n_phys = n_used + (n_used + 3) // 4
    page_table = jax.random.permutation(ks[0], n_phys)[:n_used].reshape(DEC_BATCH, n_pages).astype(jnp.int32)
    u = jax.random.uniform(ks[13], (DEPTH, WB), jnp.float32, 0.9, 0.999)
    s = u ** (1.0 / LRU_C)
    lru_lambda = jnp.log(s) - jnp.log1p(-s)
    sb_bias = jnp.linspace(SB_BIAS_HI, SB_BIAS_LO, HA, dtype=jnp.float32)[None, :] + _normal(ks[35], (DEPTH, HA), 0.1)
    return {
        "x_prompt": _normal(ks[1], (BATCH, SEQ, D_MODEL), 1.0),
        "x_sample": _normal(ks[2], (DEC_BATCH, DEC_SEQ, D_MODEL), 1.0),
        "cache_k": _normal(ks[3], (DEPTH, n_phys, PAGE_SIZE, HA, DA), 1.0),
        "cache_v": _normal(ks[4], (DEPTH, n_phys, PAGE_SIZE, HA, DA), 1.0),
        "state_lru_h": _normal(ks[5], (DEPTH, DEC_BATCH, WB), 0.5),
        "state_lru_conv": _normal(ks[6], (DEPTH, DEC_BATCH, CONV_B - 1, WB), 1.0),
        "state_conf_conv": _normal(ks[7], (DEPTH, DEC_BATCH, CONV_C - 1, WC), 1.0),
        "page_table": page_table,
        "w_in": _normal(ks[8], (DEPTH, D_MODEL, D_IN), D_MODEL ** -0.5),
        "b_merge": _normal(ks[9], (DEPTH, N_BRANCH, D_MODEL), 0.1),
        "sb_bias": sb_bias,
        "lru_conv_w": _normal(ks[10], (DEPTH, CONV_B, WB), CONV_B ** -0.5),
        "lru_conv_b": _normal(ks[11], (DEPTH, WB), 0.02),
        "lru_wa": _normal(ks[12], (DEPTH, NBLK_B, BB, BB), BB ** -0.5),
        "lru_ba": _normal(ks[14], (DEPTH, WB), 0.1),
        "lru_wx": _normal(ks[15], (DEPTH, NBLK_B, BB, BB), BB ** -0.5),
        "lru_bx": _normal(ks[16], (DEPTH, WB), 0.1),
        "lru_lambda": lru_lambda,
        "conf_conv_w": _normal(ks[17], (DEPTH, CONV_C, WC), CONV_C ** -0.5),
        "conf_conv_b": _normal(ks[18], (DEPTH, WC), 0.02),
        "conf_ln_g": 1.0 + _normal(ks[19], (DEPTH, WC), 0.05),
        "conf_ln_b": _normal(ks[20], (DEPTH, WC), 0.02),
        "w_branch": _normal(ks[21], (DEPTH, N_BRANCH, BRANCH_W, D_MODEL), BRANCH_W ** -0.5),
        "w_out": _normal(ks[22], (DEPTH, D_MODEL, D_MODEL), D_MODEL ** -0.5 * DN_BETA),
        "ln1_g": 1.0 + _normal(ks[23], (DEPTH, D_MODEL), 0.05),
        "ln1_b": _normal(ks[24], (DEPTH, D_MODEL), 0.02),
        "router_w": _normal(ks[25], (DEPTH, D_MODEL, N_EXPERTS), D_MODEL ** -0.5),
        "router_b": _normal(ks[26], (DEPTH, N_EXPERTS), 0.01),
        "moe_w_gate": _normal(ks[27], (DEPTH, N_EXPERTS, D_MODEL, D_FF), D_MODEL ** -0.5),
        "moe_b_gate": _normal(ks[28], (DEPTH, N_EXPERTS, D_FF), 0.02),
        "moe_w_up": _normal(ks[29], (DEPTH, N_EXPERTS, D_MODEL, D_FF), D_MODEL ** -0.5),
        "moe_b_up": _normal(ks[30], (DEPTH, N_EXPERTS, D_FF), 0.02),
        "moe_w_down": _normal(ks[31], (DEPTH, N_EXPERTS, D_FF, D_MODEL), D_FF ** -0.5 * DN_BETA),
        "moe_b_down": _normal(ks[32], (DEPTH, N_EXPERTS, D_MODEL), 0.02),
        "ln2_g": 1.0 + _normal(ks[33], (DEPTH, D_MODEL), 0.05),
        "ln2_b": _normal(ks[34], (DEPTH, D_MODEL), 0.02),
    }

def reference(x_prompt, x_sample, cache_k, cache_v, state_lru_h, state_lru_conv, state_conf_conv, page_table,
              w_in, b_merge, sb_bias, lru_conv_w, lru_conv_b, lru_wa, lru_ba, lru_wx, lru_bx, lru_lambda,
              conf_conv_w, conf_conv_b, conf_ln_g, conf_ln_b, w_branch, w_out, ln1_g, ln1_b,
              router_w, router_b, moe_w_gate, moe_b_gate, moe_w_up, moe_b_up, moe_w_down, moe_b_down,
              ln2_g, ln2_b):
    xp, xs = x_prompt, x_sample
    bp = xp.shape[0]
    kp, vp, ksm, vsm, hp, hsm, lcp, lcs, ccp, ccs = ([] for _ in range(10))
    for l in range(DEPTH):
        lw = (w_in[l], b_merge[l], sb_bias[l], lru_conv_w[l], lru_conv_b[l], lru_wa[l], lru_ba[l], lru_wx[l],
              lru_bx[l], lru_lambda[l], conf_conv_w[l], conf_conv_b[l], conf_ln_g[l], conf_ln_b[l], w_branch[l],
              w_out[l], ln1_g[l], ln1_b[l], router_w[l], router_b[l], moe_w_gate[l], moe_b_gate[l], moe_w_up[l],
              moe_b_up[l], moe_w_down[l], moe_b_down[l], ln2_g[l], ln2_b[l])
        xp, k, v, h, lb, cb = trunk_layer(
            xp, sb_prompt, jnp.zeros((bp, WB), xp.dtype), jnp.zeros((bp, CONV_B - 1, WB), xp.dtype),
            jnp.zeros((bp, CONV_C - 1, WC), xp.dtype), *lw)
        kp.append(k); vp.append(v); hp.append(h); lcp.append(lb); ccp.append(cb)
        attend = functools.partial(sb_sample, k_past=gather_pages(cache_k[l], page_table),
                                   v_past=gather_pages(cache_v[l], page_table))
        xs, k, v, h, lb, cb = trunk_layer(xs, attend, state_lru_h[l], state_lru_conv[l], state_conf_conv[l], *lw)
        ksm.append(k); vsm.append(v); hsm.append(h); lcs.append(lb); ccs.append(cb)
    return (xp, xs, jnp.stack(kp), jnp.stack(vp), jnp.stack(ksm), jnp.stack(vsm), jnp.stack(hp), jnp.stack(hsm),
            jnp.stack(lcp), jnp.stack(lcs), jnp.stack(ccp), jnp.stack(ccs))


_drawn_inputs = setup_inputs


def setup_inputs(seed=0):
    import zlib

    import numpy as np

    out = dict(_drawn_inputs(seed))
    spreads = {}
    factors = {'lru_ba': 2.772,
     'conf_conv_b': 3.812,
     'conf_ln_g': 2.676,
     'conf_ln_b': 6.295,
     'router_b': 3.761,
     'moe_b_gate': 8.0,
     'moe_b_up': 8.0,
     'moe_b_down': 6.431,
     'ln2_b': 2.855,
     'cache_k': 4.378,
     'cache_v': 3.51}
    for name, (base, spread) in spreads.items():
        noise = np.random.default_rng([zlib.crc32(name.encode()), seed]).standard_normal(out[name].shape)
        drawn = base * np.exp(spread * noise) if base else spread * noise
        out[name] = __import__('jax').numpy.asarray(drawn.astype(out[name].dtype))
    for name, factor in factors.items():
        out[name] = (out[name] * factor).astype(out[name].dtype)
    return out
```

```python
from contextlib import contextmanager

import concourse.bass as bass
from concourse import mybir

ALU = mybir.AluOpType
ACT = mybir.ActivationFunctionType
AX = mybir.AxisListType.X
F32, F32R, BF16 = mybir.dt.float32, mybir.dt.float32r, mybir.dt.bfloat16
I32, U32 = mybir.dt.int32, mybir.dt.uint32

P = 128
D = 1024
KT = D // P
SEQ, DEC = 512, 8
NT = SEQ + DEC
HALF = NT // 2
TT = SEQ // P + 1
W = 512
WT = W // P
HA, DA = 8, 64
NPAGE, PAGE = 16, 128
CB, CC = 4, 31
NE, TOPK = 32, 4
ALPHA = 2.0 ** 0.25
EPS = 1e-5
POOL_TAPS = 16
CHUNK = 2048
NB_EXTRA = 16
NBLK = NE + NB_EXTRA
BIG = 3.0e38

R_CW, R_CB, R_BA, R_BX, R_LAM, R_FW, R_FB, R_G, R_B = 0, 4, 5, 6, 7, 8, 39, 40, 41
R_H0, R_LBUF, R_BM, R_END = 42, 50, 74, 80
REST = {0: (512, 384), 2: (896, 128), 1: (1024, 256)}
ZW = 1280


class Port:

    def __init__(self, eng, sem, base=None):
        self.eng, self.sem, self.base = eng, sem, base or {}
        self.count, self.coef, self.i = {}, {}, None

    def at(self, name, v):
        c = self.coef.get(name, 0)
        if c == 0 and v <= 0:
            return 0
        v = max(v, 0) + self.base.get(name, 0)
        return self.i * c + v if c else v

    def now(self, name, back=0):
        return self.at(name, self.count.get(name, 0) - back)

    def next(self, name, n=1, back=0):
        self.count[name] = self.count.get(name, 0) + n
        return self.now(name, back)

    def tick(self, name, n=1):
        self.count[name] = self.count.get(name, 0) + n
        return n

    @contextmanager
    def loop(self, n, **per):
        with self.eng.Fori(0, n) as i:
            before, self.i, self.coef = dict(self.count), i, per
            yield i
            moved = {k: v - before.get(k, 0) for k, v in self.count.items() if v != before.get(k, 0)}
            assert all(per.get(k) == v for k, v in moved.items()), moved
        self.count = {k: before.get(k, 0) + n * per.get(k, 0) for k in self.count}
        self.coef, self.i = {}, None


def layout(nc):
    b = (nc.sbuf_base + 31) // 32 * 32
    t = {}

    def at(name, shape, dtype, offset):
        t[name] = nc.alloc_sbuf_tensor_at(name, [P, *shape], dtype, offset=b + offset)
        size = 2 if dtype == BF16 else 4
        for n in shape:
            size *= n
        return (offset + size + 31) // 32 * 32

    o = at("raw", [2, CHUNK], F32, 0)
    o = at("hi", [2, CHUNK], F32R, o)
    o = at("lo", [2, CHUNK], F32R, o)
    o_act = o
    o = at("act_hi", [KT, NT], F32R, o)
    o = at("act_lo", [KT, NT], F32R, o)
    o_br = o
    o = at("ob_hi", [WT, NT], F32R, o)
    o = at("ob_lo", [WT, NT], F32R, o)
    o_oc = o
    o = at("oc_hi", [WT, NT], F32R, o)
    o_cc = o
    o = at("oc_lo", [WT, NT], F32R, o)
    o_qkv = o
    o = at("qkv", [3 * WT, NT], F32, o)
    o_page = o
    o = at("page", [2, 2, W], F32, o)
    o = at("prm", [WT, R_END], F32, o)
    o = at("cbuf", [2, WT, 120], F32, o)
    o_q = o
    o = at("qb", [DEC, W], F32, o)
    o = at("zs", [DEC, NPAGE * HA], F32, o)
    o_att = o
    o = at("zb", [ZW], F32, o)
    o = at("tp", [ZW], F32, o)
    o = at("sp", [ZW], F32, o)
    o_cur = o
    o = at("qcur", [SEQ], F32, o)
    o = at("kcur", [SEQ], F32, o)
    o = at("vcur", [SEQ], F32, o)
    o_sg = o
    o = at("sg", [NT], F32, o)
    o = at("lx", [CB - 1 + NT], F32, o)
    o = at("fpad", [CC - 1 + NT], F32, o)
    o_wblk = o
    o = at("wblk", [WT, 2, P], F32, o)
    o = at("wcur", [2, P], F32, o)
    o_const = o
    for n in ("ident", "tri", "ones", "mask01", "maskbig"):
        o = at(n, [P], F32, o)
    o = at("selrow", [16], F32, o)
    o = at("sbb", [HA], F32, o)
    o = at("bm", [3 * KT], F32, o)
    o = at("c8", [WT], F32, o)
    o = at("small", [6, WT], F32, o)
    o = at("tail", [WT, 60], F32, o)
    o = at("pt", [P], I32, o)
    o_end = o
    at("xn", [TT, D], F32, o_q)
    o = at("prow", [W], F32, o_att)
    at("crow", [2, W], F32, o)
    at("tap", [SEQ], F32, o_q + W * 4)
    at("nat", [5, W], F32, o_att)
    o = o_oc
    for n in ("xc", "ga", "gi", "gel"):
        o = at(n, [NT], F32, o)
    at("cc", [WT, NT], F32, o_cc)
    at("tnat", [W], F32, o_wblk)
    at("merged", [KT, NT], F32, o_qkv + WT * NT * 4)
    at("heads", [W], F32, o_q + 2 * W * 4)
    at("late", [4, W], F32, o_q + 4 * W * 4)
    at("sgm", [2, NT], F32, o_sg)
    at("tmpm", [NT], F32, o_cur)
    o = at("mu", [NT], F32, o_att)
    o = at("sq", [2, NT], F32, o)
    at("ovs", [W], F32, o)
    at("otmp", [NT], F32, o + 2048)
    at("x1", [TT, D], F32, o_br)
    assert b + o_end <= nc.sbuf_usable_end, (b, o_end)

    o = at("mhi", [4, CHUNK], F32R, 0)
    o = at("mlo", [4, CHUNK], F32R, o)
    o_xt = o
    o = at("xt_hi", [KT, P], F32R, o)
    o = at("xt_lo", [KT, P], F32R, o)
    o = at("ht_hi", [KT, P], F32R, o)
    o = at("ht_lo", [KT, P], F32R, o)
    assert o <= o_br
    at("x1t", [2, KT, P], F32, o_xt)
    o = o_br + TT * D * 4
    o = at("mraw", [6, CHUNK], F32, o)
    o_x = o
    o = at("xrow", [D], F32, o)
    o = at("gm", [D], F32, o)
    o = at("um", [D], F32, o)
    o = at("sg_m", [D], F32, o)
    o = at("yrow", [D], F32, o)
    at("b_raw", [3 * D], F32, o_x)
    o = at("bb", [3 * D], BF16, o)
    o = at("ln_g", [D], F32, o)
    o = at("ln_b", [D], F32, o)
    o = at("rw", [KT, NE], F32, o)
    o = at("rb", [NE], F32, o)
    o = at("iota_i", [P], I32, o)
    o = at("iota_c", [P], F32, o)
    o = at("eye", [NE + 1], F32, o)
    o = at("sel_gu", [P], BF16, o)
    o = at("sel_d", [P], BF16, o)
    o = at("tid_i", [2 * TT], I32, o)
    o = at("tid", [TT, 2], BF16, o)
    o = at("ones_b", [P], BF16, o)
    o = at("before_b", [P], BF16, o)
    o = at("mv", [TT, 2], F32, o)
    o = at("rs", [TT], F32, o)
    o = at("lg", [TT, NE], F32, o)
    o = at("tv", [TT, 8], F32, o)
    o = at("ti", [TT, 8], U32, o)
    o = at("tf", [TT * TOPK], F32, o)
    o = at("wk", [TT, TOPK], F32, o)
    o = at("wsum", [TT], F32, o)
    o = at("oh", [TT, TOPK, NE], F32, o)
    o = at("ohp", [TT, TOPK, NE], F32, o)
    o = at("mm", [2, TT, NE], F32, o)
    o = at("mb", [TT, NE], BF16, o)
    o = at("rank", [TT, NE], F32, o)
    o = at("rankm", [TT, NE + 1], F32, o)
    o = at("pos", [TT, NE], F32, o)
    for n in ("cnt", "xe", "xinc", "e128", "over", "diff"):
        o = at(n, [NE], F32, o)
    at("stats", [TT, 4, 6], F32, o)
    o = at("xle", [2, NB_EXTRA, NE], F32, o)
    o = at("ej", [2, NB_EXTRA], F32, o)
    o = at("m128", [NB_EXTRA], F32, o)
    o = at("ints", [32], I32, o)
    o = at("posf", [TT * TOPK], F32, o)
    o = at("posu", [TT * TOPK], U32, o)
    o = at("eq", [TT, P], BF16, o)
    o = at("rcur", [TT], F32, o)
    o = at("mark", [2], F32, o)
    o = at("idx", [1], U32, o)
    at("yg", [2, TOPK, D], F32, 0)
    assert o <= o_const, (o, o_const)
    return t


def build(nc, a, out):
    t = layout(nc)
    ps = nc.alloc_psum_tensor("ps", [P, 8 * 512], F32)
    PAIR = [ps[:, g * 1024:(g + 1) * 1024] for g in range(4)]
    VALUES, ROWS = ps[0:HA, 3072:3584], ps[0:DEC, 3584:4096]
    ident8 = t["ident"][0:HA, 0:HA].rearrange("p (h o) -> p h o", o=1)
    Z, O = ps[:, 2048:2048 + 1536], ps[:, 3584:4096]
    sems = {}

    def sem(name):
        name = name.replace("o_", "m_", 1) if name.startswith("o_") else name
        if name not in sems:
            sems[name] = nc.alloc_semaphore(name)
        return sems[name]

    def halves(pair):
        return pair.rearrange("p (b n) -> p b n", b=2)[:, :, 0:HALF]

    def two(ap):
        return ap.rearrange("p (b n) -> p b n", b=2)

    x1d = nc.dram_tensor("x1_rows", (NT, D), F32).ap()
    yd = nc.dram_tensor("expert_rows", (NBLK * P, D), F32).ap()
    pages_k = a["cache_k"][0].rearrange("g p h d -> g p (h d)")
    pages_v = a["cache_v"][0].rearrange("g p h d -> g p (h d)")
    w_in = a["w_in"][0].rearrange("(k p) n -> p k n", p=P)
    w_br = a["w_branch"][0].rearrange("i (k p) n -> i p k n", p=P)
    w_out = a["w_out"][0].rearrange("(k p) n -> p k n", p=P)
    Q0, K0, V0, LX0, LG0, FA0, FB0, G0 = 0, W, 2 * W, 3 * W, 4 * W, 5 * W, 6 * W, 7 * W

    FREE = {"r_ready": 1, "i_ready": 1, "o_ready": 1, "exponent_ready": 1}

    def sync_program(e):
        p = Port(e, sem)

        def weights(s, *parts):
            e.wait_ge(sem("hi_ready"), p.now("hi_ready", 1))
            e.wait_ge(sem("lo_ready"), p.now("lo_ready", 1))
            o = 0
            n = sum(x.shape[2] for x in parts)
            for src in parts:
                dst = t["raw"][:, s, 0:src.shape[1] * n].rearrange("p (k n) -> p k n", n=n)[:, :, o:o + src.shape[2]]
                e.dma_start(dst, src).then_inc(sem(f"raw_full{s}"), p.tick(f"raw_full{s}", 16))
                o += src.shape[2]
            p.count["hi_ready"] = p.count.get("hi_ready", 0) + 1
            p.count["lo_ready"] = p.count.get("lo_ready", 0) + 1

        def cols(c, n=256):
            return w_in[:, :, bass.ds(c, n)]

        e.dma_start(t["xn"][:, 0:4, :], a["x_prompt"][0].rearrange("(t p) n -> p t n", p=P)).then_inc(sem("rows_moved"), p.tick("rows_moved", 16))
        e.dma_start(t["xn"][0:DEC, 4, :], a["x_sample"][:, 0, :]).then_inc(sem("rows_moved"), p.tick("rows_moved", 16))
        weights(0, cols(Q0))
        weights(1, cols(Q0 + 256))
        for i in range(2):
            weights(0, cols((i + 1) * W))
            weights(1, cols((i + 1) * W + 256))
        for i in range(4):
            weights(0, cols(i * P + LX0, P), cols(i * P + LG0, P))
            weights(1, cols(i * P + FA0, P), cols(i * P + FB0, P))
        for br in (1, 2, 0):
            for i in range(4):
                weights(0, cols(i * 256 + (G0 + br * D)))
                weights(1, w_br[br][:, :, bass.ds(i * 256, 256)])
        weights(0, w_out[:, :, 0:256])
        weights(1, w_out[:, :, 256:512])
        e.wait_ge(sem("branch_projected"), p.next("branch_projected", 24))
        e.dma_start(t["x1"][:, 0:4, :], a["x_prompt"][0].rearrange("(t p) n -> p t n", p=P)).then_inc(
            sem("rows_moved"), p.tick("rows_moved", 16))
        e.dma_start(t["x1"][0:DEC, 4, :], a["x_sample"][:, 0, :]).then_inc(sem("rows_moved"), p.tick("rows_moved", 16))
        weights(0, w_out[:, :, 512:768])
        weights(1, w_out[:, :, 768:1024])

    def scalar_dense(e):
        p = Port(e, sem, FREE)

        def act(dst, src, f=ACT.Copy, says="act_step", **kw):
            return e.activation(dst, src, f, **kw).then_inc(sem(says), p.tick(says))

        for name in ("r_ready", "i_ready", "o_ready"):
            e.nop().then_inc(sem(name), 1)
        r = 0
        for n, k in [("lru_conv_w", CB), ("lru_conv_b", 1), ("lru_ba", 1), ("lru_bx", 1), ("lru_lambda", 1),
                     ("conf_conv_w", CC), ("conf_conv_b", 1), ("conf_ln_g", 1), ("conf_ln_b", 1)]:
            e.dma_start(t["prow"][r:r + k, :], a[n][0] if k > 1 else a[n]).then_inc(sem("params_in"), p.tick("params_in", 16))
            r += k
        e.dma_start(t["prow"][R_H0:R_LBUF, :], a["state_lru_h"][0]).then_inc(sem("params_in"), p.tick("params_in", 16))
        e.dma_start(t["prow"][R_LBUF:R_BM, :], a["state_lru_conv"][0].rearrange("b j n -> (b j) n")).then_inc(sem("params_in"), p.tick("params_in", 16))
        e.dma_start(t["prow"][R_BM:R_END, :], a["b_merge"][0].rearrange("i (h n) -> (i h) n", h=2)).then_inc(sem("params_in"), p.tick("params_in", 16))
        for h in range(2):
            e.dma_start(t["crow"][0:120, h, :],
                                           a["state_conf_conv"][0, 4 * h:4 * h + 4].rearrange("b j n -> (b j) n")).then_inc(sem("params_in"), p.tick("params_in", 16))
        e.dma_start(t["sbb"][:, :], a["sb_bias"].to_broadcast([P, HA])).then_inc(sem("params_in"), p.tick("params_in", 16))
        e.dma_start(t["pt"][0:1, :], a["page_table"].rearrange("b g -> (b g)").rearrange("(o n) -> o n", o=1)).then_inc(sem("params_in"), p.tick("params_in", 16))

        chunk = [0]

        def split(n=CHUNK, dmas=1):
            s = chunk[0] % 2
            e.wait_ge(sem(f"raw_full{s}"), p.next(f"raw_full{s}", 16 * dmas))
            chunk[0] += 1
            act(t["hi"][:, s, 0:n], t["raw"][:, s, 0:n], says="hi_ready")

        e.wait_ge(sem("params_transposed"), p.next("params_transposed"))
        prm_t = PAIR[0][:, 0:WT * R_END].rearrange("p (t r) -> p t r", t=WT)
        act(t["prm"][:, :, :], prm_t)
        act(t["small"][:, 0, :].rearrange("p (t o) -> p t o", o=1), prm_t[:, :, R_LAM:R_LAM + 1], ACT.Abs, "params_ready")
        e.wait_ge(sem("params_transposed"), p.next("params_transposed"))
        act(t["cbuf"][:, :, :, :].rearrange("p h t r -> p h (t r)"),
            PAIR[1].rearrange("p (b n) -> p b n", b=2)[:, :, 0:480], says="states_ready")
        for k in range(KT):
            e.wait_ge(sem("x_transposed"), p.next("x_transposed"))
            act(t["act_hi"][:, k, :], PAIR[(k + 2) % 4][:, 0:NT], says="xhi_ready")
            if k == 1:
                split()
                split()
        e.wait_ge(sem("params_ready"), p.now("params_ready"))
        act(t["small"][:, 1, :], t["small"][:, 0, :], ACT.Exp, "explam_ready", scale=-1.0)
        for b in range(3):
            act(t["bm"][:, b * KT:(b + 1) * KT].rearrange("p (h t) -> p h t", h=2),
                t["prm"][:, :, R_BM + 2 * b:R_BM + 2 * b + 2].rearrange("p t h -> p h t"))

        step = [0]

        def load_pages(pages, row, pair):
            s = step[0] % 2
            step[0] += 1
            if step[0] > 2:
                e.wait_ge(sem("page_free"), p.next("page_free"))
            for j in range(2):
                n = row * NPAGE + pair * 2 + j
                n = e.value_load(t["pt"][0:1, n:n + 1], min_val=0, max_val=pages.shape[0] - 1)
                e.dma_start(t["page"][:, s, j, :],
                                                   pages[bass.ds(n, 1), :, :].rearrange("g p n -> p (g n)")).then_inc(sem(f"page_full{s}"), p.tick(f"page_full{s}", 16))

        for n in range(WT):
            e.wait_ge(sem("qkv_projected"), p.next("qkv_projected"))
            act(two(t["qkv"][:, n, :]), halves(PAIR[n % 2]), says="qkv_ready")
            if n % 2 == 1:
                split()
        e.wait_ge(sem("params_in"), p.now("params_in"))
        load_pages(pages_k, 0, 0)
        load_pages(pages_k, 0, 1)
        for b in range(DEC):
            e.wait_ge(sem("qb_product"), p.next("qb_product"))
            act(t["qb"][:, b, :], PAIR[2 + b % 2][:, 0:W], says="qb_ready")
        for i in range(2):
            for n in range(WT):
                e.wait_ge(sem("qkv_projected"), p.next("qkv_projected"))
                act(two(t["qkv"][:, (i + 1) * WT + n, :]), halves(PAIR[n % 2]), says="qkv_ready")
                for pr in [[(2,), (3, 4), (5,), (6, 7)], [(0, 1), (2, 3), (4, 5), (6, 7)]][i][n]:
                    load_pages(pages_k, i, pr)
                if n % 2 == 1:
                    split(dmas=1 + i)
        for u in range(2 * TT):
            n = P if u // 2 < 4 else DEC
            e.wait_ge(sem("rows_transposed"), p.next("rows_transposed"))
            if u >= 5:
                e.wait_ge(sem(f"rows_out{u % 5}"), p.next(f"rows_out{u % 5}", 16))
            act(t["nat"][0:n, u % 5, :], PAIR[u % 2][0:n, 0:W], says="rows_ready")
        for u in range(5):
            e.wait_ge(sem(f"rows_out{u}"), p.next(f"rows_out{u}", 16))

        def head(h):
            e.wait_ge(sem("z_product"), p.next("z_product"))
            act(t["zb"][:, :], Z[:, 0:ZW], ACT.Identity, "z_read", scale=DA ** -0.5, bias=t["sbb"][:, h:h + 1])
            e.wait_ge(sem("z_read"), p.now("z_read"))
            act(t["tp"][:, :], t["zb"][:, :], ACT.Abs)
            e.wait_ge(sem("act_step"), p.now("act_step"))
            act(t["tp"][:, :], t["tp"][:, :], ACT.Exp, scale=-1.0)
            e.wait_ge(sem("act_step"), p.now("act_step"))
            act(t["tp"][:, :], t["tp"][:, :], ACT.Ln, "softplus_part", bias=1.0)

        def head_weights():
            e.wait_ge(sem("exponent_ready"), p.next("exponent_ready"))
            act(t["tp"][:, :], t["zb"][:, :], ACT.Exp, "weights_ready")

        def root():
            e.wait_ge(sem("root_argument_ready"), p.next("root_argument_ready"))
            act(t["lx"][:, CB - 1:CB - 1 + NT], t["lx"][:, CB - 1:CB - 1 + NT], ACT.Sqrt, "root_ready", scale=-1.0)

        def branch_rounded(g):
            e.wait_ge(sem("branch_ready"), p.next("branch_ready"))
            act(t["ob_hi"][:, g, :], t["gel"][:, :], says="ob_hi_ready")

        for g in range(WT):
            st = [(2 + j // 2, 2 * g + j % 2) for j in range(12)]
            prm = t["prm"][:, g, :]
            load_pages(pages_k, *st[0])
            load_pages(pages_k, *st[1])
            e.wait_ge(sem("v_transposed"), p.next("v_transposed"))
            act(t["vcur"][:, :], PAIR[0][:, 0:W], says="vcur_ready")
            head(2 * g)
            if g:
                root()
            load_pages(pages_k, *st[2])
            if g:
                branch_rounded(g - 1)
            e.wait_ge(sem("lx_projected"), p.next("lx_projected"))
            act(t["lx"][:, CB - 1:CB - 1 + NT].rearrange("p (b n) -> p b n", b=2), halves(PAIR[0]), says="lx_ready")
            head_weights()
            load_pages(pages_k, *st[3])
            e.wait_ge(sem("lg_projected"), p.next("lg_projected"))
            if g:
                e.wait_ge(sem("ob_lo_ready"), p.next("ob_lo_ready"))
            act(two(t["gel"][:, :]), halves(PAIR[1]), ACT.Gelu_apprx_tanh, "gelu_ready")
            load_pages(pages_k, *st[4])
            split(dmas=2 if g < 3 else 1)
            load_pages(pages_k, *st[5])
            head(2 * g + 1)
            load_pages(pages_k, *st[6])
            load_pages(pages_k, *st[7])
            head_weights()
            e.wait_ge(sem("fb_projected"), p.next("fb_projected"))
            act(two(t["sg"][:, :]), halves(PAIR[1]), ACT.Sigmoid, "glu_gate_ready")
            load_pages(pages_k, *st[8])
            split(n=CHUNK if g < 3 else 1024, dmas=2 if g < 3 else 1)
            load_pages(pages_k, *st[9])
            e.wait_ge(sem("head_done"), p.next("head_done", 2))
            act(t["qkv"][:, g, 0:SEQ], O, says="o_ready")
            if g == 0:
                e.wait_ge(sem("c8_ready"), p.next("c8_ready"))
            e.wait_ge(sem("r_product"), p.next("r_product"))
            act(two(t["ga"][:, :]), halves(PAIR[0]), ACT.Sigmoid, "r_ready", bias=prm[:, R_BA:R_BA + 1])
            e.wait_ge(sem("i_product"), p.next("i_product"))
            act(two(t["gi"][:, :]), halves(PAIR[1]), ACT.Sigmoid, "i_ready", bias=prm[:, R_BX:R_BX + 1])
            e.wait_ge(sem("r_ready"), p.now("r_ready"))
            act(t["lx"][:, CB - 1:CB - 1 + NT], t["ga"][:, :], ACT.Tanh, scale=t["c8"][:, g:g + 1])
            act(t["ga"][:, :], t["ga"][:, :], ACT.Exp, "decay_ready", scale=t["c8"][:, g:g + 1])
            load_pages(pages_k, *st[10])
            load_pages(pages_k, *st[11])
        root()
        branch_rounded(WT - 1)
        e.wait_ge(sem("tails_transposed"), p.next("tails_transposed"))
        act(t["tnat"][0:58, :], PAIR[0][0:58, 0:W], says="tails_ready")

        turn = [0]

        def merge_turn(br, m, row=None, last=False):
            for j in range(2):
                e.wait_ge(sem("gates_projected"), p.next("gates_projected"))
                if turn[0]:
                    e.wait_ge(sem("gated"), p.next("gated"))
                act(two(t["sgm"][:, j, :]), halves(PAIR[j]), ACT.Sigmoid, "merge_gate_ready",
                    bias=t["bm"][:, br * KT + 2 * m + j:br * KT + 2 * m + j + 1])
            turn[0] += 1
            if row is not None:
                load_values(4 * row + 2)
            split()
            if row is not None:
                load_values(4 * row + 3)
            e.wait_ge(sem("branch_projected"), p.next("branch_projected", 2))
            if row is not None:
                load_values(4 * row + 4)
            if not last:
                split(n=1024)
            if row is not None:
                load_values(4 * row + 5)

        def load_values(step):
            s = step % 2
            if step >= 2:
                e.wait_ge(sem("values_used"), p.next("values_used"))
            for j in range(4):
                n = 4 * step + j
                n = e.value_load(t["pt"][0:1, n:n + 1], min_val=0, max_val=pages_v.shape[0] - 1)
                dst = t["page"][:, j // 2, j % 2, :] if s == 0 else t["late"][:, j, :]
                e.dma_start(dst, pages_v[bass.ds(n, 1), :, :].rearrange("g p n -> p (g n)")).then_inc(
                    sem(f"page_full{s}"), p.tick(f"page_full{s}", 16))

        e.wait_ge(sem("sample_scored"), p.next("sample_scored"))
        act(t["tp"][:, 0:1024], t["zb"][:, 0:1024], ACT.Abs)
        e.wait_ge(sem("act_step"), p.now("act_step"))
        act(t["tp"][:, 0:1024], t["tp"][:, 0:1024], ACT.Exp, scale=-1.0)
        e.wait_ge(sem("act_step"), p.now("act_step"))
        act(t["tp"][:, 0:1024], t["tp"][:, 0:1024], ACT.Ln, "sample_softplus_part", bias=1.0)
        merge_turn(1, 0)
        e.wait_ge(sem("sample_exponent_ready"), p.next("sample_exponent_ready"))
        act(t["zs"][:, :, :], t["zb"][:, 0:1024].rearrange("p (b n) -> p b n", b=DEC), ACT.Exp, "sample_weights_ready")
        e.wait_ge(sem("page_free"), p.next("page_free", 2))
        load_values(0)
        load_values(1)
        merge_turn(1, 1, 0)
        merge_turn(1, 2, 1)
        for j in range(WT):
            e.wait_ge(sem("centred"), p.next("centred"))
            if j >= 2:
                e.wait_ge(sem("squares_summed"), p.next("squares_summed"))
            act(t["sq"][:, j % 2, :], t["cc"][:, j, :], ACT.Square, "squares_ready")
        e.wait_ge(sem("inverse_variance_ready"), p.next("inverse_variance_ready"))
        act(t["mu"][:, :], t["mu"][:, :], ACT.Sqrt, "inverse_deviation_ready")
        for j in range(WT):
            e.wait_ge(sem("normed"), p.next("normed"))
            if j < 2:
                e.wait_ge(sem("squares_summed"), p.next("squares_summed"))
            else:
                e.wait_ge(sem("oc_lo_ready"), p.next("oc_lo_ready"))
            act(t["sq"][:, j % 2, :], t["cc"][:, j, :], ACT.Silu, scale=t["prm"][:, j, R_G:R_G + 1],
                bias=t["prm"][:, j, R_B:R_B + 1])
            e.wait_ge(sem("act_step"), p.now("act_step"))
            act(t["oc_hi"][:, j, :], t["sq"][:, j % 2, :], says="oc_hi_ready")
        merge_turn(1, 3, 2)
        for m in range(4):
            merge_turn(2, m, 3 + m)
        load_values(30)
        load_values(31)
        e.wait_ge(sem("sample_rows_product"), p.next("sample_rows_product"))
        act(t["ovs"][0:DEC, :], ROWS, says="sample_rows_ready")
        e.wait_ge(sem("oa_ready"), p.next("oa_ready"))
        act(t["ob_hi"][:, :, :], t["qkv"][:, 0:WT, :], says="ob_hi_ready")
        for m in range(4):
            merge_turn(0, m, last=m == 3)
        e.wait_ge(sem("merged_ready"), p.next("merged_ready"))
        for k in range(KT):
            act(t["act_hi"][:, k, :], t["merged"][:, k, :], says="merged_hi_ready")
        split()
        e.wait_ge(sem("out_projected"), p.next("out_projected", TT))
        split()
        e.wait_ge(sem("out_projected"), p.next("out_projected", TT))
        split()
        return p

    def vector_dense(e):
        p = Port(e, sem, FREE)

        def tt(dst, x, y, op, says="dve_step"):
            return e.tensor_tensor(dst, x, y, op).then_inc(sem(says), p.tick(says))

        def stt(dst, x, s, y, op0, op1, says="dve_step"):
            return e.scalar_tensor_tensor(out=dst, in0=x, scalar=s, in1=y, op0=op0, op1=op1).then_inc(sem(says), p.tick(says))

        def ts(dst, x, s0, op0, s1=None, op1=None, says="dve_step"):
            return (e.tensor_scalar(dst, x, s0, s1, op0, op1) if op1 else e.tensor_scalar(dst, x, s0, None, op0)).then_inc(sem(says), p.tick(says))

        def copy(dst, src, says="dve_step"):
            return e.tensor_copy(dst, src).then_inc(sem(says), p.tick(says))

        chunk = [0]

        def split(n=CHUNK, used=None, times=1):
            s = chunk[0] % 2
            if used:
                e.wait_ge(sem(used), p.next(used, times))
            e.wait_ge(sem("hi_ready"), p.next("hi_ready"))
            chunk[0] += 1
            tt(t["lo"][:, s, 0:n], t["raw"][:, s, 0:n], t["hi"][:, s, 0:n].bitcast(F32), ALU.subtract, "lo_ready")

        step = [0]

        def score(row, pair):
            s = step[0] % 2
            step[0] += 1
            e.wait_ge(sem(f"page_full{s}"), p.next(f"page_full{s}", 32))
            kp = t["page"][:, s, :, :]
            tt(kp, kp, t["qb"][:, row:row + 1, :].to_broadcast([P, 2, W]), ALU.mult)
            e.wait_ge(sem("dve_step"), p.now("dve_step"))
            e.tensor_reduce(t["zs"][:, row, pair * 16:pair * 16 + 16],
                                             kp.rearrange("p j (h d) -> p (j h) d", d=DA), axis=AX, op=ALU.add).then_inc(sem("page_free"), p.tick("page_free"))

        e.nop().then_inc(sem("exponent_ready"), 1)
        for k in range(KT):
            e.wait_ge(sem("xhi_ready"), p.next("xhi_ready"))
            tt(t["act_lo"][:, k, :], PAIR[(k + 2) % 4][:, 0:NT], t["act_hi"][:, k, :].bitcast(F32), ALU.subtract, "xlo_ready")
            if k == 1:
                split()
                split()
        e.wait_ge(sem("explam_ready"), p.next("explam_ready"))
        sm = t["small"]
        ts(sm[:, 2, :], sm[:, 1, :], 2.0, ALU.add)
        e.wait_ge(sem("dve_step"), p.now("dve_step"))
        e.reciprocal(sm[:, 2, :], sm[:, 2, :]).then_inc(sem("dve_step"), p.tick("dve_step"))
        e.wait_ge(sem("dve_step"), p.now("dve_step"))
        tt(sm[:, 2, :], sm[:, 2, :], sm[:, 1, :], ALU.mult)
        e.wait_ge(sem("dve_step"), p.now("dve_step"))
        tt(sm[:, 3, :], sm[:, 2, :], sm[:, 2, :], ALU.mult)
        e.wait_ge(sem("dve_step"), p.now("dve_step"))
        ts(sm[:, 4, :], sm[:, 3, :], 1.0 / 17, ALU.mult)
        e.wait_ge(sem("dve_step"), p.now("dve_step"))
        for n in (15, 13, 11, 9, 7, 5, 3):
            stt(sm[:, 4, :], sm[:, 4, :], 1.0 / n, sm[:, 3, :], ALU.add, ALU.mult)
            e.wait_ge(sem("dve_step"), p.now("dve_step"))
        stt(sm[:, 4, :], sm[:, 4, :], 1.0, sm[:, 2, :], ALU.add, ALU.mult)
        ts(sm[:, 5, :].rearrange("p (t o) -> p t o", o=1), t["prm"][:, :, R_LAM:R_LAM + 1], 0.0, ALU.min, 8.0, ALU.mult)
        e.wait_ge(sem("dve_step"), p.now("dve_step"))
        stt(t["c8"][:, :], sm[:, 4, :], -16.0, sm[:, 5, :], ALU.mult, ALU.add, "c8_ready")
        split(used="qkv_projected", times=2)
        split(used="qkv_projected", times=2)
        e.wait_ge(sem("qb_ready"), p.next("qb_ready", DEC))
        for i in range(2):
            for pair in range(8):
                score(i, pair)
                if pair in (3, 7):
                    split(used="qkv_projected", times=2)

        def diagonal(x):
            return x[:, 0:SEQ].rearrange("p (b n) -> p b n", b=4)

        def block_mask(m):
            return t[m][:, :].rearrange("p (o n) -> p o n", o=1).to_broadcast([P, 4, P])

        def head_softplus():
            e.wait_ge(sem("softplus_part"), p.next("softplus_part"))
            stt(t["sp"][:, :], t["zb"][:, :], 0.0, t["tp"][:, :], ALU.max, ALU.add)
            e.wait_ge(sem("dve_step"), p.now("dve_step"))
            tt(diagonal(t["sp"]), diagonal(t["sp"]), block_mask("mask01"), ALU.mult, "softplus_ready")

        def head_exponent():
            e.wait_ge(sem("suffix_product"), p.next("suffix_product"))
            tt(t["zb"][:, :], t["zb"][:, :], Z[:, 0:ZW], ALU.subtract)
            e.wait_ge(sem("dve_step"), p.now("dve_step"))
            tt(diagonal(t["zb"]), diagonal(t["zb"]), block_mask("maskbig"), ALU.min, "exponent_ready")

        def later_taps(g, part):
            if part == 0:
                e.wait_ge(sem("conv_done"), p.next("conv_done"))
            cc = t["cc"][:, g, 0:SEQ]
            half = (POOL_TAPS + CC) // 2
            for j in range(POOL_TAPS, half) if part == 0 else range(half, CC):
                stt(cc, t["fpad"][:, j:j + SEQ], t["prm"][:, g, R_FW + j:R_FW + j + 1], cc, ALU.mult, ALU.add)
                e.wait_ge(sem("dve_step"), p.now("dve_step"))

        def copy_heads(g):
            if g:
                e.wait_ge(sem("head_done"), p.next("head_done", 2))
            copy(t["qcur"][:, :], t["qkv"][:, g, 0:SEQ])
            copy(t["kcur"][:, :], t["qkv"][:, WT + g, 0:SEQ])
            copy(t["sg"][:, 0:SEQ], t["qkv"][:, 2 * WT + g, 0:SEQ], "heads_copied")

        LX = t["lx"][:, CB - 1:CB - 1 + NT]

        def recurrence(g):
            prm = t["prm"][:, g, :]
            e.wait_ge(sem("root_ready"), p.next("root_ready"))
            tt(t["gi"][:, :], LX, t["gi"][:, :], ALU.mult)
            e.wait_ge(sem("dve_step"), p.now("dve_step"))
            e.tensor_tensor_scan(t["xc"][:, 0:SEQ], t["ga"][:, 0:SEQ], t["gi"][:, 0:SEQ], 0.0, ALU.mult, ALU.add).then_inc(
                sem("dve_step"), p.tick("dve_step"))
            tt(t["xc"][:, SEQ:NT], t["ga"][:, SEQ:NT], prm[:, R_H0:R_LBUF], ALU.mult)
            e.wait_ge(sem("dve_step"), p.now("dve_step"))
            tt(t["xc"][:, SEQ:NT], t["xc"][:, SEQ:NT], t["gi"][:, SEQ:NT], ALU.add)
            e.wait_ge(sem("dve_step"), p.now("dve_step"))
            copy(t["tail"][:, g, 49:58], t["xc"][:, SEQ - 1:NT], "tail_gathered")
            e.wait_ge(sem("gelu_ready"), p.next("gelu_ready"))
            tt(t["gel"][:, :], t["gel"][:, :], t["xc"][:, :], ALU.mult, "branch_ready")
            e.wait_ge(sem("ob_hi_ready"), p.next("ob_hi_ready"))
            tt(t["ob_lo"][:, g, :], t["gel"][:, :], t["ob_hi"][:, g, :].bitcast(F32), ALU.subtract, "ob_lo_ready")

        e.wait_ge(sem("qkv_ready"), p.next("qkv_ready", 3 * WT))
        e.wait_ge(sem("constants_ready"), p.next("constants_ready"))
        e.wait_ge(sem("gate_blocks_in"), p.next("gate_blocks_in", 64))
        copy(t["wcur"][:, :, :], t["wblk"][:, 0, :, :])
        copy_heads(0)
        for g in range(WT):
            prm = t["prm"][:, g, :]
            st = [(2 + j // 2, 2 * g + j % 2) for j in range(12)]
            score(*st[0])
            score(*st[1])
            head_softplus()
            score(*st[2])
            head_exponent()
            if g:
                recurrence(g - 1)
            score(*st[3])
            e.wait_ge(sem("lx_ready"), p.next("lx_ready"))
            ts(t["xc"][:, 0:SEQ], t["lx"][:, 0:SEQ], prm[:, R_CW:R_CW + 1], ALU.mult, prm[:, R_CB:R_CB + 1], ALU.add)
            lb = prm[:, R_LBUF:R_BM].rearrange("p (b j) -> p j b", j=CB - 1)
            ts(t["xc"][:, SEQ:NT], lb[:, 0, :], prm[:, R_CW:R_CW + 1], ALU.mult, prm[:, R_CB:R_CB + 1], ALU.add)
            copy(t["tail"][:, g, 0:11], t["lx"][:, SEQ:SEQ + 11])
            e.wait_ge(sem("dve_step"), p.now("dve_step"))
            for j in range(1, CB):
                w = prm[:, R_CW + j:R_CW + j + 1]
                stt(t["xc"][:, 0:SEQ], t["lx"][:, j:j + SEQ], w, t["xc"][:, 0:SEQ], ALU.mult, ALU.add)
                stt(t["xc"][:, SEQ:NT], lb[:, j, :] if j < CB - 1 else t["lx"][:, CB - 1 + SEQ:CB - 1 + NT], w,
                    t["xc"][:, SEQ:NT], ALU.mult, ALU.add, "dve_step" if j < CB - 1 else "rg_input_ready")
                e.wait_ge(sem("dve_step"), p.now("dve_step"))
            split(used="lg_projected")
            if g:
                later_taps(g - 1, 0)
            score(*st[4])
            score(*st[5])
            head_softplus()
            score(*st[6])
            score(*st[7])
            head_exponent()
            if g:
                later_taps(g - 1, 1)
            e.wait_ge(sem("glu_gate_ready"), p.next("glu_gate_ready"))
            e.wait_ge(sem("fa_projected"), p.next("fa_projected"))
            tt(two(t["fpad"][:, CC - 1:CC - 1 + NT]), halves(PAIR[0]), two(t["sg"][:, :]), ALU.mult, "glu_ready")
            e.wait_ge(sem("glu_ready"), p.now("glu_ready"))
            copy(t["tail"][:, g, 11:49], t["fpad"][:, SEQ:SEQ + 38])
            score(*st[8])
            split(CHUNK if g < 3 else 1024, used="fb_projected")
            score(*st[9])
            if g < WT - 1:
                copy_heads(g + 1)
            e.wait_ge(sem("i_ready"), p.next("i_ready"))
            if g < WT - 1:
                copy(t["wcur"][:, :, :], t["wblk"][:, g + 1, :, :])
            tt(t["gi"][:, :], t["gi"][:, :], t["xc"][:, :], ALU.mult)
            e.wait_ge(sem("decay_ready"), p.next("decay_ready"))
            e.wait_ge(sem("dve_step"), p.now("dve_step"))
            tt(t["xc"][:, :], t["ga"][:, :], t["ga"][:, :], ALU.mult)
            e.wait_ge(sem("dve_step"), p.now("dve_step"))
            stt(LX, t["xc"][:, :], 1.0, LX, ALU.add, ALU.mult, "root_argument_ready")
            score(*st[10])
            score(*st[11])
        recurrence(WT - 1)

        e.wait_ge(sem("page_free"), p.now("page_free"))
        e.wait_ge(sem("head_done"), p.next("head_done", 2))
        zf = t["zb"][:, 0:1024]
        stt(zf.rearrange("p (n h) -> p n h", h=HA), t["zs"][:, :, :].rearrange("p b (g h) -> p (b g) h", h=HA), DA ** -0.5,
            t["sbb"][:, :].rearrange("p (o h) -> p o h", o=1).to_broadcast([P, DEC * NPAGE, HA]), ALU.mult, ALU.add,
            "sample_scored")
        e.wait_ge(sem("sample_softplus_part"), p.next("sample_softplus_part"))
        stt(t["sp"][:, 0:1024], zf, 0.0, t["tp"][:, 0:1024], ALU.max, ALU.add, "sample_softplus_ready")

        def merge_turn(br, m, last=False):
            split(used="gates_projected", times=2)
            for j in range(2):
                e.wait_ge(sem("branch_projected"), p.next("branch_projected"))
                e.wait_ge(sem("merge_gate_ready"), p.next("merge_gate_ready"))
                dst = t["merged"][:, 2 * m + j, :]
                first = br == 1
                if not first or j or m:
                    e.wait_ge(sem("dve_step"), p.now("dve_step"))
                tt(two(dst if first else t["tmpm"][:, :]), halves(PAIR[2 - j]), two(t["sgm"][:, j, :]), ALU.mult, "gated")
                if not first:
                    e.wait_ge(sem("gated"), p.now("gated"))
                    tt(dst, dst, t["tmpm"][:, :], ALU.add, "merged_ready" if last and j else "dve_step")
            if not last:
                split(1024)

        def own_channels(row):
            e.wait_ge(sem("values_used"), p.next("values_used", 4))
            own = ident8.to_broadcast([DEC, HA, DA])
            tt(t["heads"][0:HA, :].rearrange("p (h d) -> p h d", h=HA), VALUES.rearrange("p (h d) -> p h d", h=HA), own, ALU.mult,
               "row_ready")

        merge_turn(1, 0)
        e.wait_ge(sem("sample_sums"), p.next("sample_sums"))
        later = t["tp"][:, 0:1024].rearrange("p (b g h) -> p g b h", b=DEC, h=HA)
        sums = PAIR[3].rearrange("p (b g h) -> p g b h", b=DEC, h=HA)
        e.memset(later[:, NPAGE - 1, :, :], 0.0).then_inc(sem("dve_step"), p.tick("dve_step"))
        e.wait_ge(sem("dve_step"), p.now("dve_step"))
        for g in range(NPAGE - 2, -1, -1):
            tt(later[:, g, :, :], later[:, g + 1, :, :], sums[:, g + 1, :, :], ALU.add)
            e.wait_ge(sem("dve_step"), p.now("dve_step"))
        tt(zf, zf, t["tp"][:, 0:1024], ALU.subtract, "sample_sums_read")
        e.wait_ge(sem("sample_sums_read"), p.now("sample_sums_read"))
        e.wait_ge(sem("sample_sums"), p.next("sample_sums"))
        tt(zf, zf, PAIR[2][:, 0:1024], ALU.subtract, "sample_exponent_ready")
        for g in range(WT):
            for h in range(2):
                cb = t["cbuf"][:, h, g, :].rearrange("p (b j) -> p b j", j=CC - 1)
                tt(cb, cb, t["prm"][:, g:g + 1, R_FW:R_FW + CC - 1].to_broadcast([P, 4, CC - 1]), ALU.mult)
        later_taps(WT - 1, 0)
        later_taps(WT - 1, 1)
        for g in range(WT):
            for h in range(2):
                e.tensor_reduce(t["tmpm"][:, g * 8 + h * 4:g * 8 + h * 4 + 4],
                                                t["cbuf"][:, h, g, :].rearrange("p (b j) -> p b j", j=CC - 1), axis=AX, op=ALU.add).then_inc(sem("dve_step"), p.tick("dve_step"))
        e.wait_ge(sem("dve_step"), p.now("dve_step"))
        for g in range(WT):
            c = t["cc"][:, g, SEQ:NT]
            tt(c, c, t["tmpm"][:, g * 8:g * 8 + 8], ALU.add, "conv_ready")
        merge_turn(1, 1)
        own_channels(0)
        e.wait_ge(sem("channel_sum"), p.next("channel_sum"))
        ts(two(t["mu"][:, :]), halves(PAIR[2]), 1.0 / W, ALU.mult, says="mean_ready")
        e.wait_ge(sem("mean_ready"), p.now("mean_ready"))
        for j in range(WT):
            tt(t["cc"][:, j, :], t["cc"][:, j, :], t["mu"][:, :], ALU.subtract, "centred")
        merge_turn(1, 2)
        own_channels(1)
        e.wait_ge(sem("squares_summed"), p.next("squares_summed", WT))
        e.wait_ge(sem("centred"), p.now("centred"))
        ts(two(t["mu"][:, :]), halves(PAIR[2]), 1.0 / W, ALU.mult, EPS, ALU.add, says="variance_ready")
        e.wait_ge(sem("variance_ready"), p.now("variance_ready"))
        e.reciprocal(t["mu"][:, :], t["mu"][:, :]).then_inc(sem("inverse_variance_ready"), p.tick("inverse_variance_ready"))
        e.wait_ge(sem("inverse_deviation_ready"), p.next("inverse_deviation_ready"))
        for j in range(WT):
            tt(t["cc"][:, j, :], t["cc"][:, j, :], t["mu"][:, :], ALU.mult, "normed")
        for j in range(WT):
            e.wait_ge(sem("oc_hi_ready"), p.next("oc_hi_ready"))
            tt(t["oc_lo"][:, j, :], t["sq"][:, j % 2, :], t["oc_hi"][:, j, :].bitcast(F32), ALU.subtract, "oc_lo_ready")
        merge_turn(1, 3)
        own_channels(2)
        for m in range(4):
            merge_turn(2, m)
            own_channels(3 + m)
        own_channels(7)
        e.wait_ge(sem("sample_rows_transposed"), p.next("sample_rows_transposed"))
        copy(t["qkv"][:, 0:WT, SEQ:NT], PAIR[0][:, 0:WT * DEC].rearrange("p (t b) -> p t b", t=WT), "oa_ready")
        e.wait_ge(sem("ob_hi_ready"), p.next("ob_hi_ready"))
        tt(t["ob_lo"][:, :, :], t["qkv"][:, 0:WT, :], t["ob_hi"][:, :, :].bitcast(F32), ALU.subtract, "ob_lo_ready")
        for m in range(4):
            merge_turn(0, m, last=m == 3)
        for k in range(KT):
            e.wait_ge(sem("merged_hi_ready"), p.next("merged_hi_ready"))
            tt(t["act_lo"][:, k, :], t["merged"][:, k, :], t["act_hi"][:, k, :].bitcast(F32), ALU.subtract, "merged_lo_ready")
        split()
        for _ in range(2):
            e.nop().then_inc(sem("residual_ready"), p.tick("residual_ready"))
        e.wait_ge(sem("rows_moved"), p.next("rows_moved", 64))
        for c in range(4):
            if c in (1, 2):
                split()
            for i in range(TT):
                n = P if i < 4 else DEC
                e.wait_ge(sem("out_projected"), p.next("out_projected"))
                x = t["x1"][0:n, i, c * 256:(c + 1) * 256]
                stt(x, x, ALPHA, PAIR[(c * TT + i) % 2][0:n, 0:256], ALU.mult, ALU.add, "residual_ready")
                e.wait_ge(sem("residual_ready"), p.now("residual_ready"))
                e.bn_stats(t["stats"][0:n, i, c, :], x).then_inc(sem("dve_step"), p.tick("dve_step"))
        return p

    def tensor_dense(e):
        p = Port(e, sem, FREE)
        ident = t["ident"][:, :]

        def three(out, lhi, llo, rhi, rlo, start, stop):
            e.matmul(out, lhi, rhi, start=start, stop=False)
            e.matmul(out, lhi, rlo, start=False, stop=False)
            return e.matmul(out, llo, rhi, start=False, stop=stop)

        def project(pair, s, j, says, n=256, kt=KT, act=("act_hi", "act_lo")):
            hi, lo = (t[x][:, s, 0:kt * n].rearrange("p (k n) -> p k n", n=n)[:, :, j * P:(j + 1) * P] for x in ("hi", "lo"))
            ahi, alo = t[act[0]], t[act[1]]
            for k in range(kt):
                for h in range(2):
                    c = slice(h * HALF, (h + 1) * HALF)
                    last = three(PAIR[pair][:, h * 512:h * 512 + HALF], hi[:, k, :], lo[:, k, :], ahi[:, k, c], alo[:, k, c],
                                 k == 0, k == kt - 1)
            return last.then_inc(sem(says), p.tick(says))

        def next_chunk():
            e.wait_ge(sem("hi_ready"), p.next("hi_ready"))
            e.wait_ge(sem("lo_ready"), p.next("lo_ready"))

        e.wait_ge(sem("constants_ready"), p.next("constants_ready"))
        e.wait_ge(sem("params_in"), p.next("params_in", 16 * 16))
        for k in range(WT):
            last = e.transpose(PAIR[0][:, k * R_END:(k + 1) * R_END], t["prow"][0:R_END, k * P:(k + 1) * P], ident[0:R_END, 0:R_END])
        last.then_inc(sem("params_transposed"), p.tick("params_transposed"))
        for h in range(2):
            for k in range(WT):
                last = e.transpose(PAIR[1][:, h * 512 + k * 120:h * 512 + (k + 1) * 120], t["crow"][0:120, h, k * P:(k + 1) * P],
                                   ident[0:120, 0:120])
        last.then_inc(sem("params_transposed"), p.tick("params_transposed"))
        e.wait_ge(sem("rows_moved"), p.next("rows_moved", 32))
        for k in range(KT):
            if k == 2:
                e.wait_ge(sem("params_ready"), p.next("params_ready"))
            if k == 3:
                e.wait_ge(sem("states_ready"), p.next("states_ready"))
            if k >= 4:
                e.wait_ge(sem("xlo_ready"), p.next("xlo_ready"))
            for i in range(TT):
                n = P if i < 4 else DEC
                last = e.transpose(PAIR[(k + 2) % 4][:, i * P:i * P + n], t["xn"][0:n, i, k * P:(k + 1) * P], ident[0:n, 0:n])
            last.then_inc(sem("x_transposed"), p.tick("x_transposed"))
        e.wait_ge(sem("xlo_ready"), p.next("xlo_ready", 4))
        for c in range(2):
            next_chunk()
            for j in range(2):
                if c:
                    e.wait_ge(sem("qkv_ready"), p.next("qkv_ready"))
                last = project(j, c, j, "qkv_projected")
        e.wait_ge(sem("qkv_ready"), p.next("qkv_ready", 2))
        for b in range(DEC):
            if b >= 2:
                e.wait_ge(sem("qb_ready"), p.next("qb_ready"))
            for k in range(WT):
                col = t["qkv"][:, k, SEQ + b:SEQ + b + 1].to_broadcast([P, P])
                last = e.matmul(PAIR[2 + b % 2][:, k * P:(k + 1) * P], col, ident, start=True, stop=True)
            last.then_inc(sem("qb_product"), p.tick("qb_product"))
        with p.loop(2, hi_ready=2, lo_ready=2, qkv_ready=4, qkv_projected=4):
            for c in range(2):
                next_chunk()
                for j in range(2):
                    e.wait_ge(sem("qkv_ready"), p.now("qkv_ready", 1))
                    p.count["qkv_ready"] += 1
                    project(j, c, j, "qkv_projected")
        e.wait_ge(sem("qkv_ready"), p.next("qkv_ready", 0))
        for u in range(2 * TT):
            n = P if u // 2 < 4 else DEC
            if u >= 2:
                e.wait_ge(sem("rows_ready"), p.next("rows_ready"))
            for k in range(WT):
                src = t["qkv"][:, (1 + u % 2) * WT + k, u // 2 * P:u // 2 * P + n]
                last = e.transpose(PAIR[u % 2][0:n, k * P:(k + 1) * P], src, ident)
            last.then_inc(sem("rows_transposed"), p.tick("rows_transposed"))
        e.wait_ge(sem("rows_ready"), p.next("rows_ready", 2))
        e.wait_ge(sem("qb_ready"), p.next("qb_ready", 2))
        def scores(par):
            r = slice(par * DA, (par + 1) * DA)
            for kb in range(4):
                q0 = kb * P
                e.matmul(Z[:, q0:q0 + P], t["kcur"][r, q0:q0 + P], t["qcur"][r, q0:q0 + P], start=True, stop=True)
            for kb, (o, n) in REST.items():
                last = e.matmul(Z[:, o:o + n], t["kcur"][r, kb * P:(kb + 1) * P], t["qcur"][r, (kb + 1) * P:SEQ],
                                start=True, stop=True)
            last.then_inc(sem("z_product"), p.tick("z_product"))

        def suffixes():
            sp = t["sp"]
            e.wait_ge(sem("softplus_ready"), p.next("softplus_ready"))
            e.matmul(Z[:, 0:SEQ], t["tri"][:, :], sp[:, 0:SEQ], start=True, stop=True)
            for kb, (o, n) in REST.items():
                parts = [(t["tri"], o, 0, n)]
                for later in range(kb + 1, 4):
                    parts.append((t["ones"], later * P, (later - kb - 1) * P, P))
                    if later < 3:
                        parts.append((t["ones"], REST[later][0], (later - kb) * P, REST[later][1]))
                for x, (m, src, dst, w) in enumerate(parts):
                    last = e.matmul(Z[:, o + dst:o + dst + w], m[:, :], sp[:, src:src + w], start=x == 0, stop=x == len(parts) - 1)
            last.then_inc(sem("suffix_product"), p.tick("suffix_product"))

        def outputs(par):
            e.wait_ge(sem("weights_ready"), p.next("weights_ready"))
            out = O[par * DA:(par + 1) * DA, :]
            for kb in range(4):
                v = t["vcur"][:, kb * P + par * DA:kb * P + (par + 1) * DA]
                last = e.matmul(out[:, kb * P:(kb + 1) * P], v, t["tp"][:, kb * P:(kb + 1) * P], start=kb == 0, stop=kb == 3)
                if kb < 3:
                    o, n = REST[kb]
                    e.matmul(out[:, (kb + 1) * P:SEQ], v, t["tp"][:, o:o + n], start=False, stop=False)
            last.then_inc(sem("head_done"), p.tick("head_done"))

        with p.loop(4, heads_copied=1, r_ready=1, v_transposed=1, exponent_ready=2, z_product=2, hi_ready=2, lo_ready=2,
                    vcur_ready=1, lx_projected=1, softplus_ready=2, suffix_product=2, i_ready=1, lg_projected=1, o_ready=1,
                    weights_ready=2, head_done=2, lx_ready=1, fa_projected=1, gelu_ready=1, fb_projected=1,
                    glu_ready=1, rg_input_ready=1, r_product=1, glu_gate_ready=1, i_product=1, z_read=2):
            e.wait_ge(sem("heads_copied"), p.next("heads_copied"))
            e.wait_ge(sem("r_ready"), p.now("r_ready"))
            for k in range(4):
                last = e.transpose(PAIR[0][:, k * P:(k + 1) * P], t["sg"][:, k * P:(k + 1) * P], ident)
            last.then_inc(sem("v_transposed"), p.tick("v_transposed"))
            e.wait_ge(sem("exponent_ready"), p.now("exponent_ready"))
            scores(0)
            next_chunk()
            e.wait_ge(sem("vcur_ready"), p.next("vcur_ready"))
            project(0, 0, 0, "lx_projected")
            e.wait_ge(sem("z_read"), p.next("z_read"))
            suffixes()
            e.wait_ge(sem("i_ready"), p.now("i_ready"))
            project(1, 0, 1, "lg_projected")
            e.wait_ge(sem("o_ready"), p.now("o_ready"))
            outputs(0)
            e.wait_ge(sem("exponent_ready"), p.next("exponent_ready"))
            scores(1)
            next_chunk()
            e.wait_ge(sem("lx_ready"), p.next("lx_ready"))
            project(0, 1, 0, "fa_projected")
            e.wait_ge(sem("z_read"), p.next("z_read"))
            suffixes()
            e.wait_ge(sem("gelu_ready"), p.next("gelu_ready"))
            project(1, 1, 1, "fb_projected")
            outputs(1)
            e.wait_ge(sem("glu_ready"), p.next("glu_ready"))
            e.wait_ge(sem("rg_input_ready"), p.next("rg_input_ready"))
            for h in range(2):
                c = slice(h * HALF, (h + 1) * HALF)
                last = e.matmul(PAIR[0][:, h * 512:h * 512 + HALF], t["wcur"][:, 0, :], t["xc"][:, c], start=True, stop=True)
            last.then_inc(sem("r_product"), p.tick("r_product"))
            e.wait_ge(sem("glu_gate_ready"), p.next("glu_gate_ready"))
            for h in range(2):
                c = slice(h * HALF, (h + 1) * HALF)
                last = e.matmul(PAIR[1][:, h * 512:h * 512 + HALF], t["wcur"][:, 1, :], t["xc"][:, c], start=True, stop=True)
            last.then_inc(sem("i_product"), p.tick("i_product"))
            for name in ("r_ready", "i_ready", "o_ready", "exponent_ready"):
                p.count[name] = p.count.get(name, 0) + 1
        e.wait_ge(sem("tail_gathered"), p.next("tail_gathered", 4))
        e.wait_ge(sem("r_ready"), p.now("r_ready"))
        for k in range(WT):
            last = e.transpose(PAIR[0][0:58, k * P:(k + 1) * P], t["tail"][:, k, 0:58], ident)
        last.then_inc(sem("tails_transposed"), p.tick("tails_transposed"))
        e.wait_ge(sem("i_ready"), p.now("i_ready"))
        e.wait_ge(sem("o_ready"), p.now("o_ready"))
        e.wait_ge(sem("exponent_ready"), p.now("exponent_ready"))
        e.wait_ge(sem("tails_ready"), p.next("tails_ready"))

        def merge_turn(act, row=None, free=()):
            next_chunk()
            e.wait_ge(sem("merge_gate_ready"), p.now("merge_gate_ready"))
            project(0, 0, 0, "gates_projected")
            if row is not None:
                add_values(4 * row)
            e.wait_ge(sem("gated"), p.now("gated"))
            project(1, 0, 1, "gates_projected")
            if row is not None:
                add_values(4 * row + 1)
            next_chunk()
            for name in free:
                e.wait_ge(sem(name), p.next(name))
            project(2, 1, 0, "branch_projected", kt=WT, act=act)
            if row is not None:
                add_values(4 * row + 2)
            e.wait_ge(sem("merge_gate_ready"), p.next("merge_gate_ready", 2))
            project(1, 1, 1, "branch_projected", kt=WT, act=act)
            if row is not None:
                add_values(4 * row + 3)
            p.count["gated"] = p.count.get("gated", 0) + 2

        for s in range(2):
            p.count[f"page_full{s}"] = 32 * 32

        def add_values(step):
            row, s = step // 4, step % 2
            if step == 0:
                e.wait_ge(sem("sample_weights_ready"), p.next("sample_weights_ready"))
            if step and step % 4 == 0:
                add_row(row - 1)
            e.wait_ge(sem(f"page_full{s}"), p.next(f"page_full{s}", 64))
            for j in range(4):
                g = step % 4 * 4 + j
                v = t["page"][:, j // 2, j % 2, :] if s == 0 else t["late"][:, j, :]
                last = e.matmul(VALUES, t["zs"][:, row, g * HA:(g + 1) * HA], v, start=g == 0, stop=g == NPAGE - 1)
            last.then_inc(sem("values_used"), p.tick("values_used"))

        def add_row(row):
            e.wait_ge(sem("row_ready"), p.next("row_ready"))
            return e.matmul(ROWS, t["selrow"][0:HA, 7 - row:15 - row], t["heads"][0:HA, :], start=row == 0, stop=row == DEC - 1)

        def over_channels(pair, src, m, says, first=True, last=True):
            for h in range(2):
                c = slice(h * HALF, (h + 1) * HALF)
                x = e.matmul(PAIR[pair][:, h * 512:h * 512 + HALF], m, src[:, c], start=first, stop=last)
            return x.then_inc(sem(says), p.tick(says)) if says else x

        B, C, A = (("ob_hi", "ob_lo"), ("oc_hi", "oc_lo"), ("ob_hi", "ob_lo"))
        e.wait_ge(sem("ob_lo_ready"), p.next("ob_lo_ready", 4))
        merge_turn(B)
        e.wait_ge(sem("gated"), p.now("gated"))
        e.wait_ge(sem("sample_softplus_ready"), p.next("sample_softplus_ready"))
        for h in range(2):
            last = e.matmul(PAIR[3][:, h * 512:(h + 1) * 512], t["ones"][:, :], t["sp"][:, h * 512:(h + 1) * 512], start=True, stop=True)
        last.then_inc(sem("sample_sums"), p.tick("sample_sums"))
        for h in range(2):
            last = e.matmul(PAIR[2][:, h * 512:(h + 1) * 512], t["tri"][:, :], t["sp"][:, h * 512:(h + 1) * 512], start=True, stop=True)
        last.then_inc(sem("sample_sums"), p.tick("sample_sums"))

        merge_turn(B, 0, ("sample_sums_read", "sample_exponent_ready"))
        e.wait_ge(sem("gated"), p.now("gated"))
        e.wait_ge(sem("conv_ready"), p.next("conv_ready", WT))
        for k in range(WT):
            over_channels(2, t["cc"][:, k, :], t["ones"][:, :], "channel_sum" if k == WT - 1 else None, k == 0, k == WT - 1)
        merge_turn(B, 1, ("mean_ready",))
        e.wait_ge(sem("gated"), p.now("gated"))
        for k in range(WT):
            e.wait_ge(sem("squares_ready"), p.next("squares_ready"))
            over_channels(2, t["sq"][:, k % 2, :], t["ones"][:, :], "squares_summed", k == 0, k == WT - 1)
        merge_turn(B, 2, ("variance_ready",))
        e.wait_ge(sem("oc_lo_ready"), p.next("oc_lo_ready", 4))
        for m in range(4):
            merge_turn(C, 3 + m)
        for step in range(28, 32):
            add_values(step)
        last = add_row(DEC - 1)
        last.then_inc(sem("sample_rows_product"), p.tick("sample_rows_product"))
        e.wait_ge(sem("sample_rows_ready"), p.next("sample_rows_ready"))
        e.wait_ge(sem("merge_gate_ready"), p.now("merge_gate_ready"))
        for k in range(WT):
            last = e.transpose(PAIR[0][:, k * DEC:(k + 1) * DEC], t["ovs"][0:DEC, k * P:(k + 1) * P], ident[0:DEC, 0:DEC])
        last.then_inc(sem("sample_rows_transposed"), p.tick("sample_rows_transposed"))
        e.wait_ge(sem("ob_lo_ready"), p.next("ob_lo_ready"))
        e.wait_ge(sem("oa_ready"), p.next("oa_ready"))
        merge_turn(A)
        with p.loop(3, hi_ready=2, lo_ready=2, merge_gate_ready=2, gates_projected=2, gated=2, branch_projected=2):
            merge_turn(A)
        e.wait_ge(sem("gated"), p.now("gated"))
        e.wait_ge(sem("merged_lo_ready"), p.next("merged_lo_ready", KT))
        p.count["residual_ready"] = 1
        with p.loop(2, hi_ready=2, lo_ready=2, residual_ready=10, out_projected=10):
            for c in range(2):
                next_chunk()
                hi, lo = (t[x][:, c, :].rearrange("p (k n) -> p k n", n=256) for x in ("hi", "lo"))
                for i in range(TT):
                    n = P if i < 4 else DEC
                    r = slice(i * P, i * P + n)
                    e.wait_ge(sem("residual_ready"), p.now("residual_ready"))
                    p.count["residual_ready"] = p.count.get("residual_ready", 0) + 1
                    for k in range(KT):
                        last = three(PAIR[(c * TT + i) % 2][0:n, 0:256], t["act_hi"][:, k, r], t["act_lo"][:, k, r],
                                     hi[:, k, :], lo[:, k, :], k == 0, k == KT - 1)
                    last.then_inc(sem("out_projected"), p.tick("out_projected"))
        return p

    def gpsimd_dense(e):
        p = Port(e, sem)

        for n, v in (("ident", 0.0), ("tri", 1.0), ("ones", 1.0), ("mask01", 1.0), ("maskbig", BIG), ("selrow", 0.0)):
            e.memset(t[n][:, :], v).then_inc(sem("pool_step"), p.tick("pool_step"))
        for n, w in (("lx", CB - 1), ("fpad", CC - 1)):
            e.memset(t[n][:, 0:w], 0.0).then_inc(sem("pool_step"), p.tick("pool_step"))
        e.memset(t["wblk"][:, :, :, :], 0.0).then_inc(sem("zeros_ready"), p.tick("zeros_ready"))
        e.wait_ge(sem("zeros_ready"), p.now("zeros_ready"))
        e.wait_ge(sem("pool_step"), p.now("pool_step"))
        for w, n in enumerate(("lru_wa", "lru_wx")):
            for h in range(2):
                r = slice(h * DA, (h + 1) * DA)
                src = a[n][0].rearrange("(g r) i j -> r i g j", r=2)[h]
                e.dma_start(t["wblk"][r, :, w, r], src).then_inc(sem("gate_blocks_in"), p.tick("gate_blocks_in", 16))
        e.memset(t["selrow"][:, 7:8], 1.0).then_inc(sem("pool_step"), p.tick("pool_step"))
        for n, cm, step, base, op, fill in (("ident", 1, -1, 0, ALU.not_equal, 1.0), ("tri", 1, -1, 0, ALU.is_ge, 0.0),
                                            ("mask01", -1, 1, -1, ALU.is_ge, 0.0), ("maskbig", -1, 1, -1, ALU.is_ge, -BIG)):
            e.affine_select(out=t[n][:, :], in_=t[n][:, :], pattern=[[step, P]], compare_op=op, fill=fill,
                                             base=base, channel_multiplier=cm).then_inc(sem("pool_step"), p.tick("pool_step"))
        e.wait_ge(sem("pool_step"), p.now("pool_step"))
        e.memset(t["tail"][:, :, 58:60], 0.0).then_inc(sem("constants_ready"), p.tick("constants_ready"))
        e.dma_start(out["lru_conv_sample"][0, :, 0:CB - 2, :], a["state_lru_conv"][0, :, 1:CB - 1, :]).then_inc(sem("states_out"), p.tick("states_out", 16))
        e.dma_start(out["conf_conv_sample"][0, :, 0:CC - 2, :], a["state_conf_conv"][0, :, 1:CC - 1, :]).then_inc(sem("states_out"), p.tick("states_out", 16))
        for x in range(0, NB_EXTRA, SEQ // P):
            e.dma_start(yd[(NE + x) * P:(NE + x) * P + SEQ, :], a["x_prompt"][0]).then_inc(sem("states_out"), p.tick("states_out", 16))
        for u in range(2 * TT):
            i, kv = u // 2, "kv"[u % 2]
            e.wait_ge(sem("rows_ready"), p.next("rows_ready"))
            if i < 4:
                dst = out[kv + "_prompt"][0, 0, i * P:(i + 1) * P].rearrange("p h d -> p (h d)")
            else:
                dst = out[kv + "_sample"][0, :, 0].rearrange("p h d -> p (h d)")
            e.dma_start(dst, t["nat"][0:P if i < 4 else DEC, u % 5, :]).then_inc(sem(f"rows_out{u % 5}"), p.tick(f"rows_out{u % 5}", 16))

        for g in range(WT):
            w = t["prm"][:, g, R_FW:R_FW + CC]
            bias = t["prm"][:, g, R_FB:R_FB + 1]
            cc, x = t["cc"][:, g, :], t["fpad"]
            e.wait_ge(sem("glu_ready"), p.next("glu_ready"))
            e.tensor_scalar(cc[:, 0:SEQ], x[:, 0:SEQ], w[:, 0:1], bias, ALU.mult, ALU.add).then_inc(sem("pool_step"), p.tick("pool_step"))
            e.tensor_scalar(cc[:, SEQ:NT], x[:, CC - 1 + SEQ:CC - 1 + NT], w[:, CC - 1:CC], bias, ALU.mult, ALU.add).then_inc(sem("pool_step"), p.tick("pool_step"))
            for j in range(1, POOL_TAPS):
                e.wait_ge(sem("pool_step"), p.now("pool_step"))
                e.tensor_scalar(t["tap"][:, :], x[:, j:j + SEQ], w[:, j:j + 1], None, ALU.mult).then_inc(sem("pool_step"), p.tick("pool_step"))
                e.wait_ge(sem("pool_step"), p.now("pool_step"))
                e.tensor_tensor(cc[:, 0:SEQ], cc[:, 0:SEQ], t["tap"][:, :], ALU.add).then_inc(sem("pool_step" if j < POOL_TAPS - 1 else "conv_done"), p.tick("pool_step" if j < POOL_TAPS - 1 else "conv_done"))

        e.wait_ge(sem("tails_ready"), p.next("tails_ready"))
        tn = t["tnat"]
        for dst, r, n in ((out["lru_conv_prompt"][0, 0], 0, 3), (out["lru_conv_sample"][0, :, CB - 2], 3, 8),
                          (out["conf_conv_prompt"][0, 0], 11, 30), (out["conf_conv_sample"][0, :, CC - 2], 41, 8),
                          (out["lru_h_prompt"][0], 49, 1), (out["lru_h_sample"][0], 50, 8)):
            e.dma_start(dst, tn[r:r + n, :]).then_inc(sem("states_out"), p.tick("states_out", 16))

        e.wait_ge(sem("states_out"), p.now("states_out"))
        return p


    GATE, UP, DOWN, TURN = PAIR
    WG, WU, WD = (a[n][0] for n in ("moe_w_gate", "moe_w_up", "moe_w_down"))
    ident = t["ident"][:, :]
    rows = [(i, P if i < TT - 1 else DEC) for i in range(TT)]
    RATE = {pre + n: 1 for pre in ("m_", "o_") for n in (
        "eq_ready", "idx_product", "idx_ready", "x_turned", "xt_hi", "xt_lo", "sel_gu", "sel_d", "g_read", "u_read",
        "sigmoid_ready", "h_ready", "h_turned", "ht_hi", "ht_lo", "y_ready", "passed")}
    for pre in ("m_", "o_"):
        RATE.update({pre + n: 16 for n in ("x_gathered", "y_out")})
        RATE.update({pre + f"raw{s}": 32 for s in range(6)})
        RATE.update({pre + "hi": 12, pre + "used": 12, pre + "lo_dve": 9 if pre == "m_" else 12, pre + "lo_pool": 3})
    RATE.update(m_dve=1, o_dve=2)
    BASE = {"o_" + n: NE + 1 for n in ("eq_ready", "idx_product", "idx_ready", "x_turned", "xt_hi", "xt_lo", "sel_gu",
                                     "passed")}
    BASE.update({"o_" + n: NE for n in ("sel_d", "g_read", "u_read", "sigmoid_ready", "h_ready", "h_turned", "ht_hi", "ht_lo",
                                        "y_ready", "dve")})
    BASE.update({f"o_raw{s}": 16 * 12 * NE // 6 for s in range(6)})
    BASE.update(o_x_gathered=16 * (NE + 1), o_y_out=16 * NE, o_hi=12 * NE, o_used=12 * NE, o_lo_dve=9 * NE)

    class Stream:

        def __init__(self, p, pre):
            self.p, self.pre, self.n = p, pre, 0

        def sem(self, name):
            return sem(self.pre + name)

        def at(self, name, v):
            return self.p.at(self.pre + name, v)

        def tick(self, name):
            return self.p.tick(self.pre + name)

        def split_done(self, n):
            if n < 0:
                return
            if self.pre == "m_" and n % 4 == 3:
                self.p.eng.wait_ge(self.sem("lo_pool"), self.at("lo_pool", n // 4 + 1))
            else:
                self.p.eng.wait_ge(self.sem("lo_dve"), self.at("lo_dve", n + 1 - (n + 1) // 4 if self.pre == "m_" else n + 1))

        def start(self, b):
            return 12 * b if self.pre == "o_" else (0 if b == 0 else 12 * b - 4)

    def blocks(p, pre, n):
        return p.loop(n, **{k: v for k, v in RATE.items() if k.startswith(pre)})

    def load(s, w, expert, c):
        n, slot = s.n, s.n % 6
        s.split_done(n - 6)
        src = w[bass.ds(expert, 1)].rearrange("o (k p) n -> (o p) k n", p=P)[:, 2 * c:2 * c + 2, :]
        s.p.eng.dma_start(t["mraw"][:, slot, :].rearrange("p (k n) -> p k n", k=2), src).then_inc(sem(s.pre + f"raw{slot}"), s.p.tick(s.pre + f"raw{slot}", 16))
        s.n += 1

    def sync_experts(e):
        p = Port(e, sem)
        s = Stream(p, "m_")
        for name, n in (("ln_in", 32), ("router_in", 32), ("b_in", 144)):
            e.wait_ge(sem(name), p.next(name, n))
        for b in range(2):
            for w, x in ((WG, b), (WU, b), (WD, b - 1)):
                for c in range(4 if x >= 0 else 0):
                    load(s, w, x, c)
                    if s.n == 6:
                        for i, n in rows:
                            e.wait_ge(sem("rows_normed"), p.next("rows_normed"))
                            e.dma_start(x1d[i * P:i * P + n, :], t["x1"][0:n, i, :]).then_inc(sem("rows_moved"), p.tick("rows_moved", 16))
        with blocks(p, "m_", NE - 2) as i:
            this, before = e.snap(i + 2), e.snap(i + 1)
            for w, x in ((WG, this), (WU, this), (WD, before)):
                for c in range(4):
                    load(s, w, x, c)
        s.n = s.start(NE)
        for c in range(4):
            load(s, WD, NE - 1, c)

    def sync_extra(e):
        p = Port(e, sem, BASE)
        n = e.value_load(t["ints"][0:1, 0:1], min_val=0, max_val=NB_EXTRA)
        with e.If(n > 0):
            s = Stream(p, "o_")
            with blocks(p, "o_", n) as j:
                x = e.value_load(t["ints"][0:1, bass.ds(j + 1, 1)], min_val=0, max_val=NE - 1)
                for w in (WG, WU, WD):
                    for c in range(4):
                        if s.n == 2:
                            e.wait_ge(s.sem("x_gathered"), s.at("x_gathered", 16))
                        load(s, w, x, c)

    def round_chunk(s):
        n = s.n
        s.p.eng.wait_ge(s.sem("used"), s.at("used", n - 3))
        s.p.eng.wait_ge(s.sem(f"raw{n % 6}"), s.at(f"raw{n % 6}", 16 * (n // 6 + 1)))
        s.p.eng.activation(t["mhi"][:, n % 4, :], t["mraw"][:, n % 6, :], ACT.Copy).then_inc(s.sem("hi"), s.tick("hi"))
        s.n += 1

    def round_turned(s, name, b):
        s.p.eng.wait_ge(s.sem("x_turned" if name == "xt" else "h_turned"), s.at("x_turned" if name == "xt" else "h_turned", b + 1))
        s.p.eng.activation(t[name + "_hi"][:, :, :].rearrange("p k n -> p (k n)"), TURN, ACT.Copy).then_inc(s.sem(name + "_hi"), s.tick(name + "_hi"))

    def gate_sigmoid(s, b):
        s.p.eng.wait_ge(s.sem("g_read"), s.at("g_read", b + 1))
        s.p.eng.wait_ge(s.sem("h_ready"), s.at("h_ready", b))
        s.p.eng.activation(t["sg_m"][:, :], t["gm"][:, :], ACT.Sigmoid, scale=1.702).then_inc(s.sem("sigmoid_ready"), s.tick("sigmoid_ready"))

    def rows_out(s, b, block, end):
        s.p.eng.wait_ge(s.sem("used"), s.at("used", end))
        s.p.eng.wait_ge(s.sem("y_out"), s.at("y_out", 16 * b))
        s.p.eng.activation(t["yrow"][:, :], DOWN, ACT.Copy).then_inc(s.sem("y_ready"), s.tick("y_ready"))
        s.p.eng.wait_ge(s.sem("y_ready"), s.at("y_ready", b + 1))
        s.p.eng.dma_start(yd[bass.ds(block * P, P), :], t["yrow"][:, :]).then_inc(sem(s.pre + "y_out"), s.p.tick(s.pre + "y_out", 16))

    def scalar_experts(e):
        p = Port(e, sem)

        def act(says, dst, src, f=ACT.Copy, **kw):
            return e.activation(dst, src, f, **kw).then_inc(sem(says), p.tick(says))

        for j, n in enumerate(("moe_b_gate", "moe_b_up", "moe_b_down")):
            for g in range(3):
                e.dma_start(t["b_raw"][g * NE:(g + 1) * NE, j * D:(j + 1) * D], a[n][0]).then_inc(sem("b_in"), p.tick("b_in", 16))
        e.wait_ge(sem("variance"), p.next("variance"))
        act("deviation", t["rs"][:, :], t["rs"][:, :], ACT.Sqrt)
        e.wait_ge(sem("b_in"), p.now("b_in"))
        act("bias_rounded", t["bb"][0:96, :], t["b_raw"][0:96, :])
        for i, n in rows:
            e.wait_ge(sem("x1_turned"), p.next("x1_turned"))
            if i >= 2:
                e.wait_ge(sem("logits_tile"), p.next("logits_tile"))
            act("x1t_ready", t["x1t"][:, i % 2, :, 0:n], (GATE, UP)[i % 2].rearrange("p (k n) -> p k n", k=KT)[:, :, 0:n])
        e.wait_ge(sem("bias_rest"), p.next("bias_rest"))
        act("bias_part", t["bb"][32:64, :], t["b_raw"][32:64, :])
        act("bias_rounded", t["bb"][64:96, :], t["b_raw"][64:96, :])
        s = Stream(p, "m_")
        for c in range(4):
            round_chunk(s)
            if c == 2:
                e.wait_ge(sem("bias_rest"), p.next("bias_rest"))
                act("bias_part", t["bb"][64:96, :], t["b_raw"][64:96, :])
        e.wait_ge(sem("top_centred"), p.next("top_centred"))
        act("top_exp", t["wk"][:, :, :], t["wk"][:, :, :], ACT.Exp)
        e.wait_ge(sem("logits_tile"), p.at("logits_tile", TT))
        round_turned(s, "xt", 0)

        def turn(b, block):
            if b:
                for c in range(4):
                    round_chunk(s)
                if b >= 2:
                    rows_out(s, b - 2, block, s.start(b))
            for c in range(4):
                round_chunk(s)
            if b:
                round_turned(s, "ht", b - 1)
            gate_sigmoid(s, b)
            if b:
                for c in range(4):
                    round_chunk(s)
            round_turned(s, "xt", b + 1)

        turn(0, None)
        turn(1, None)
        with blocks(p, "m_", NE - 2) as i:
            turn(2, i)
        s.n = s.start(NE)
        for c in range(4):
            round_chunk(s)
        rows_out(s, NE - 2, NE - 2, s.start(NE))
        round_turned(s, "ht", NE - 1)
        rows_out(s, NE - 1, NE - 1, s.start(NE) + 4)
        s.p.eng.wait_ge(s.sem("y_out"), s.at("y_out", 16 * NE))

    def scalar_extra(e):
        p = Port(e, sem, BASE)
        n = e.value_load(t["ints"][0:1, 0:1], min_val=0, max_val=NB_EXTRA)
        with e.If(n > 0):
            s = Stream(p, "o_")
            with blocks(p, "o_", n) as j:
                round_turned(s, "xt", 0)
                for c in range(8):
                    round_chunk(s)
                gate_sigmoid(s, 0)
                for c in range(4):
                    round_chunk(s)
                round_turned(s, "ht", 0)
                rows_out(s, 0, j + NE, 12)
                s.p.eng.wait_ge(s.sem("y_out"), s.at("y_out", 16))

    def remainder(s):
        n = s.n
        s.p.eng.wait_ge(s.sem("used"), s.at("used", n - 3))
        s.p.eng.wait_ge(s.sem("hi"), s.at("hi", n + 1))
        e, says = s.p.eng, "lo_dve" if s.pre == "o_" or n % 4 < 3 else "lo_pool"
        e.tensor_tensor(t["mlo"][:, n % 4, :], t["mraw"][:, n % 6, :], t["mhi"][:, n % 4, :].bitcast(F32), ALU.subtract).then_inc(s.sem(says), s.tick(says))
        s.n += 1

    def slots(s, b, expert, m128=None):
        e = s.p.eng
        s.p.eng.wait_ge(s.sem("idx_product"), s.at("idx_product", b))
        r = t["rankm"][:, :, bass.ds(expert, 1)]
        if m128 is not None:
            rc = t["rcur"][:, :].rearrange("p (i o) -> p i o", o=1)
            e.tensor_scalar(rc, r, m128, None, ALU.subtract).then_inc(s.sem("dve"), s.tick("dve"))
            e.wait_ge(sem(s.pre + "dve"), s.p.now(s.pre + "dve"))
            r = rc
        e.tensor_tensor(t["eq"][:, :, :], t["iota_c"][:, :].rearrange("p (o n) -> p o n", o=1).to_broadcast([P, TT, P]),
                                          r.to_broadcast([P, TT, P]), ALU.is_equal).then_inc(s.sem("eq_ready"), s.tick("eq_ready"))

    def tokens(s, b):
        s.p.eng.wait_ge(s.sem("idx_product"), s.at("idx_product", b + 1))
        s.p.eng.wait_ge(s.sem("x_gathered"), s.at("x_gathered", 16 * b))
        s.p.eng.tensor_copy(t["idx"][:, :], TURN[:, 0:1]).then_inc(s.sem("idx_ready"), s.tick("idx_ready"))

    def select(s, which, expert):
        s.p.eng.tensor_copy(t[which][0:96, :], t["eye"][0:96, bass.ds(expert, 1)].to_broadcast([96, P])).then_inc(s.sem(which), s.tick(which))

    def turned_remainder(s, name, b):
        s.p.eng.wait_ge(s.sem(name + "_hi"), s.at(name + "_hi", b + 1))
        flat = [t[name + x][:, :, :].rearrange("p k n -> p (k n)") for x in ("_lo", "_hi")]
        s.p.eng.tensor_tensor(flat[0], TURN, flat[1].bitcast(F32), ALU.subtract).then_inc(s.sem(name + "_lo"), s.tick(name + "_lo"))

    def gate_limit(s, b, end):
        s.p.eng.wait_ge(s.sem("used"), s.at("used", end))
        s.p.eng.wait_ge(s.sem("h_ready"), s.at("h_ready", b))
        s.p.eng.tensor_scalar(t["gm"][:, :], GATE, 7.0, None, ALU.min).then_inc(s.sem("g_read"), s.tick("g_read"))

    def hidden(s, b, end):
        e = s.p.eng
        s.p.eng.wait_ge(s.sem("used"), s.at("used", end))
        s.p.eng.wait_ge(s.sem("h_turned"), s.at("h_turned", b))
        e.tensor_scalar(t["um"][:, :], UP, -7.0, 7.0, ALU.max, ALU.min).then_inc(s.sem("u_read"), s.tick("u_read"))
        s.p.eng.wait_ge(s.sem("u_read"), s.at("u_read", b + 1))
        e.scalar_tensor_tensor(out=t["um"][:, :], in0=t["um"][:, :], scalar=1.0, in1=t["gm"][:, :], op0=ALU.add, op1=ALU.mult).then_inc(s.sem("dve"), s.tick("dve"))
        e.wait_ge(sem(s.pre + "dve"), s.p.now(s.pre + "dve"))
        s.p.eng.wait_ge(s.sem("sigmoid_ready"), s.at("sigmoid_ready", b + 1))
        e.tensor_tensor(t["um"][:, :], t["um"][:, :], t["sg_m"][:, :], ALU.mult).then_inc(s.sem("h_ready"), s.tick("h_ready"))

    def vector_experts(e):
        p = Port(e, sem)

        def tt(dst, x, y, op, says="dve"):
            return e.tensor_tensor(dst, x, y, op).then_inc(sem(says), p.tick(says))

        def ts(dst, x, s0, op0, s1=None, op1=None, says="dve"):
            return (e.tensor_scalar(dst, x, s0, s1, op0, op1) if op1 else e.tensor_scalar(dst, x, s0, None, op0)).then_inc(sem(says), p.tick(says))

        e.memset(t["rs"][:, :], 1.0).then_inc(sem("dve"), p.tick("dve"))
        e.memset(t["tv"][:, :, :], 0.0).then_inc(sem("dve"), p.tick("dve"))
        e.memset(t["tf"][:, :], -1.0).then_inc(sem("dve"), p.tick("dve"))
        e.memset(t["rankm"][:, :, NE:NE + 1], -1.0e6).then_inc(sem("dve"), p.tick("dve"))
        for i, n in rows:
            e.bn_aggr(t["mv"][0:n, i, :], t["stats"][0:n, i, :, :]).then_inc(sem("dve"), p.tick("dve"))
        e.wait_ge(sem("dve"), p.now("dve"))
        for i, n in rows:
            ts(t["rs"][0:n, i:i + 1], t["mv"][0:n, i, 1:2], EPS, ALU.add)
        e.wait_ge(sem("dve"), p.now("dve"))
        e.reciprocal(t["rs"][:, :], t["rs"][:, :]).then_inc(sem("variance"), p.tick("variance"))
        e.wait_ge(sem("variance"), p.now("variance"))
        e.wait_ge(sem("deviation"), p.next("deviation"))
        e.wait_ge(sem("ln_in"), p.next("ln_in", 32))
        for i, n in rows:
            x = t["x1"][0:n, i, :]
            ts(x, x, t["mv"][0:n, i, 0:1], ALU.subtract, t["rs"][0:n, i:i + 1], ALU.mult)
            e.wait_ge(sem("dve"), p.now("dve"))
            tt(x, x, t["ln_g"][0:n, :], ALU.mult)
            e.wait_ge(sem("dve"), p.now("dve"))
            tt(x, x, t["ln_b"][0:n, :], ALU.add, "rows_normed")
        e.wait_ge(sem("router_in"), p.next("router_in", 32))
        e.wait_ge(sem("logits_tile"), p.next("logits_tile", TT))
        rb = t["rb"][:, :].rearrange("p (o n) -> p o n", o=1)
        tt(t["lg"][:, 0:4, :], DOWN[:, 0:4 * NE].rearrange("p (i n) -> p i n", i=4), rb.to_broadcast([P, 4, NE]), ALU.add)
        tt(t["lg"][0:DEC, 4, :], DOWN[0:DEC, 4 * NE:5 * NE], t["rb"][0:DEC, :], ALU.add)
        e.wait_ge(sem("dve"), p.now("dve"))
        for i, n in rows:
            e.max(t["tv"][0:n, i, :], t["lg"][0:n, i, :]).then_inc(sem("dve"), p.tick("dve"))
        e.wait_ge(sem("dve"), p.now("dve"))
        for i, n in rows:
            e.max_index(t["ti"][0:n, i, :], t["tv"][0:n, i, :], t["lg"][0:n, i, :]).then_inc(sem("dve"), p.tick("dve"))
        tt(t["wk"][:, :, :], t["tv"][:, :, 0:TOPK], t["tv"][:, :, 0:1].to_broadcast([P, TT, TOPK]), ALU.subtract, "top_centred")
        e.wait_ge(sem("dve"), p.now("dve"))
        for i, n in rows:
            e.tensor_copy(t["tf"][0:n, i * TOPK:(i + 1) * TOPK], t["ti"][0:n, i, 0:TOPK]).then_inc(sem("dve"), p.tick("dve"))
        e.wait_ge(sem("dve"), p.now("dve"))
        e.wait_ge(sem("pool_constants"), p.next("pool_constants"))
        iota = t["iota_c"][:, 0:NE].rearrange("p (o n) -> p o n", o=1)
        oh = t["oh"][:, :, :, :]
        flat = oh.rearrange("p i k e -> p (i k) e")
        tt(flat, iota.to_broadcast([P, TT * TOPK, NE]), t["tf"][:, :].rearrange("p (n o) -> p n o", o=1).to_broadcast([P, TT * TOPK, NE]),
           ALU.is_equal)
        e.wait_ge(sem("dve"), p.now("dve"))
        mm = t["mm"]
        for h in range(2):
            tt(mm[:, h, :, :], oh[:, :, 2 * h, :], oh[:, :, 2 * h + 1, :], ALU.add)
        e.wait_ge(sem("dve"), p.now("dve"))
        tt(mm[:, 0, :, :], mm[:, 0, :, :], mm[:, 1, :, :], ALU.add)
        e.wait_ge(sem("dve"), p.now("dve"))
        e.tensor_copy(t["mb"][:, :, :], mm[:, 0, :, :]).then_inc(sem("chosen_ready"), p.tick("chosen_ready"))
        ts(t["e128"][:, :], t["iota_c"][:, 0:NE], float(P), ALU.mult)
        e.wait_ge(sem("rank_product"), p.next("rank_product"))
        e.tensor_copy(t["cnt"][:, :], TURN[:, 0:NE]).then_inc(sem("dve"), p.tick("dve"))
        e.tensor_copy(t["rank"][:, :, :], DOWN[:, 512:512 + TT * NE].rearrange("p (i n) -> p i n", i=TT)).then_inc(sem("dve"), p.tick("dve"))
        e.wait_ge(sem("dve"), p.now("dve"))
        e.scalar_tensor_tensor(out=t["rankm"][:, :, 0:NE], in0=t["rank"][:, :, :], scalar=1.0e6, in1=mm[:, 0, :, :], op0=ALU.add, op1=ALU.mult).then_inc(sem("dve"), p.tick("dve"))
        e.wait_ge(sem("dve"), p.now("dve"))
        ts(t["rankm"][:, :, 0:NE], t["rankm"][:, :, 0:NE], 1.0e6, ALU.subtract)
        e.wait_ge(sem("dve"), p.now("dve"))
        s = Stream(p, "m_")
        slots(s, 0, 0)
        tokens(s, 0)
        select(s, "sel_gu", 0)
        ts(t["xe"][:, :], t["cnt"][:, :], float(P), ALU.is_gt)
        e.wait_ge(sem("dve"), p.now("dve"))
        for m in range(2, TT):
            e.scalar_tensor_tensor(out=t["xe"][:, :], in0=t["cnt"][:, :], scalar=float(P * m), in1=t["xe"][:, :], op0=ALU.is_gt, op1=ALU.add).then_inc(sem("dve"), p.tick("dve"))
            e.wait_ge(sem("dve"), p.now("dve"))
        e.tensor_tensor_scan(t["xinc"][:, :], t["ones"][:, 0:NE], t["xe"][:, :], 0.0, ALU.mult, ALU.add).then_inc(sem("dve"), p.tick("dve"))
        e.wait_ge(sem("dve"), p.now("dve"))
        tt(t["over"][:, :], t["xinc"][:, :], t["xe"][:, :], ALU.subtract)
        e.wait_ge(sem("dve"), p.now("dve"))
        ts(t["over"][:, :], t["over"][:, :], float(NE - 1), ALU.add, float(P), ALU.mult)
        e.wait_ge(sem("dve"), p.now("dve"))
        tt(t["diff"][:, :], t["over"][:, :], t["e128"][:, :], ALU.subtract)
        e.wait_ge(sem("dve"), p.now("dve"))
        pos = t["pos"][:, :, :]
        b5 = lambda x: t[x][:, :].rearrange("p (o n) -> p o n", o=1).to_broadcast([P, TT, NE])
        e.scalar_tensor_tensor(out=pos, in0=t["rank"][:, :, :], scalar=float(P), in1=b5("diff"), op0=ALU.is_ge, op1=ALU.mult).then_inc(sem("dve"), p.tick("dve"))
        e.wait_ge(sem("dve"), p.now("dve"))
        tt(pos, pos, b5("e128"), ALU.add)
        e.wait_ge(sem("dve"), p.now("dve"))
        tt(pos, pos, t["rank"][:, :, :], ALU.add)
        e.wait_ge(sem("dve"), p.now("dve"))
        for k in range(TOPK):
            tt(t["ohp"][:, :, k, :], oh[:, :, k, :], pos, ALU.mult)
        e.wait_ge(sem("dve"), p.now("dve"))
        e.tensor_reduce(t["posf"][:, :], t["ohp"][:, :, :, :].rearrange("p i k e -> p (i k) e"), axis=AX, op=ALU.add).then_inc(sem("dve"), p.tick("dve"))
        e.wait_ge(sem("dve"), p.now("dve"))
        e.tensor_copy(t["posu"][:, :], t["posf"][:, :]).then_inc(sem("dve"), p.tick("dve"))
        xi = t["xinc"][:, :].rearrange("p (o n) -> p o n", o=1).to_broadcast([P, NB_EXTRA, NE])
        jj = t["iota_c"][:, 0:NB_EXTRA].rearrange("p (n o) -> p n o", o=1).to_broadcast([P, NB_EXTRA, NE])
        tt(t["xle"][:, 0, :, :], xi, jj, ALU.is_le)
        e.wait_ge(sem("dve"), p.now("dve"))
        tt(t["xle"][:, 1, :, :], t["xle"][:, 0, :, :], xi, ALU.mult)
        e.tensor_reduce(t["ej"][:, 0, :], t["xle"][:, 0, :, :], axis=AX, op=ALU.add).then_inc(sem("dve"), p.tick("dve"))
        e.wait_ge(sem("dve"), p.now("dve"))
        e.tensor_reduce(t["ej"][:, 1, :], t["xle"][:, 1, :, :], axis=AX, op=ALU.max).then_inc(sem("dve"), p.tick("dve"))
        ts(t["ej"][:, 0, :], t["ej"][:, 0, :], float(NE - 1), ALU.min)
        e.wait_ge(sem("dve"), p.now("dve"))
        tt(t["m128"][:, :], t["iota_c"][:, 0:NB_EXTRA], t["ej"][:, 1, :], ALU.subtract)
        e.tensor_copy(t["ints"][:, 0:1], t["xinc"][:, NE - 1:NE]).then_inc(sem("dve"), p.tick("dve"))
        e.tensor_copy(t["ints"][:, 1:1 + NB_EXTRA], t["ej"][:, 0, :]).then_inc(sem("dve"), p.tick("dve"))
        e.wait_ge(sem("dve"), p.now("dve"))
        ts(t["m128"][:, :], t["m128"][:, :], 1.0, ALU.add, float(P), ALU.mult)
        e.wait_ge(sem("top_exp"), p.next("top_exp"))
        e.tensor_reduce(t["wsum"][:, :], t["wk"][:, :, :], axis=AX, op=ALU.add).then_inc(sem("dve"), p.tick("dve"))
        e.wait_ge(sem("dve"), p.now("dve"))
        e.reciprocal(t["wsum"][:, :], t["wsum"][:, :]).then_inc(sem("dve"), p.tick("dve"))
        e.wait_ge(sem("dve"), p.now("dve"))
        tt(t["wk"][:, :, :], t["wk"][:, :, :], t["wsum"][:, :].rearrange("p (i o) -> p i o", o=1).to_broadcast([P, TT, TOPK]), ALU.mult)
        e.wait_ge(sem("dve"), p.now("dve"))

        turned_remainder(s, "xt", 0)

        def turn(b, e0):
            if b:
                remainder(s)
                slots(s, b + 1, e0 + 2)
                remainder(s)
                remainder(s)
                s.n += 1
                select(s, "sel_d", e0)
                tokens(s, b + 1)
            else:
                for c in range(3):
                    remainder(s)
                s.n += 1
                slots(s, 1, 1)
                tokens(s, 1)
            for c in range(3):
                remainder(s)
            s.n += 1
            gate_limit(s, b, s.start(b) + 4)
            if b:
                turned_remainder(s, "ht", b - 1)
                for c in range(3):
                    remainder(s)
                s.n += 1
            hidden(s, b, s.start(b) + 8)
            turned_remainder(s, "xt", b + 1)
            select(s, "sel_gu", e0 + 2)

        turn(0, -1)
        turn(1, 0)
        with blocks(p, "m_", NE - 2) as i:
            turn(2, i + 1)
        s.n = s.start(NE)
        for c in range(3):
            remainder(s)
        select(s, "sel_d", NE - 1)
        turned_remainder(s, "ht", NE - 1)

    def vector_extra(e):
        p = Port(e, sem, BASE)
        n = e.value_load(t["ints"][0:1, 0:1], min_val=0, max_val=NB_EXTRA)
        with e.If(n > 0):
            s = Stream(p, "o_")
            with blocks(p, "o_", n) as j:
                x = e.value_load(t["ints"][0:1, bass.ds(j + 1, 1)], min_val=0, max_val=NE - 1)
                s.p.eng.wait_ge(s.sem("used"), s.at("used", 0))
                select(s, "sel_gu", x)
                select(s, "sel_d", x)
                slots(s, 0, x, t["m128"][:, bass.ds(j, 1)])
                tokens(s, 0)
                turned_remainder(s, "xt", 0)
                for c in range(8):
                    remainder(s)
                gate_limit(s, 0, 4)
                for c in range(4):
                    remainder(s)
                hidden(s, 0, 8)
                turned_remainder(s, "ht", 0)

    def bias(e, dst, sel, which):
        for h in range(2):
            c = slice(h * 512, (h + 1) * 512)
            e.matmul(dst[:, c], t[sel][0:96, :], t["bb"][0:96, which * D + h * 512:which * D + (h + 1) * 512], start=True, stop=False)

    def multiply(s, c, dst, name):
        s.split_done(s.n)
        e, slot = s.p.eng, s.n % 4
        hi, lo = (t[x][:, slot, :] for x in ("mhi", "mlo"))
        for h in range(2):
            for k in range(2):
                cols = slice(k * D + h * 512, k * D + (h + 1) * 512)
                xh, xl = t[name + "_hi"][:, 2 * c + k, :], t[name + "_lo"][:, 2 * c + k, :]
                out = dst[:, h * 512:(h + 1) * 512]
                e.matmul(out, xh, hi[:, cols], start=False, stop=False)
                e.matmul(out, xh, lo[:, cols], start=False, stop=False)
                last = e.matmul(out, xl, hi[:, cols], start=False, stop=c == 3 and k == 1)
        last.then_inc(s.sem("used"), s.tick("used"))
        s.n += 1

    def find(s, b):
        s.p.eng.wait_ge(s.sem("eq_ready"), s.at("eq_ready", b + 1))
        e = s.p.eng
        for i in range(TT):
            for x in range(2):
                last = e.matmul(TURN[:, 0:1], t["eq"][:, i, :], t["tid"][:, i, x:x + 1], start=i + x == 0, stop=i + x == TT)
        last.then_inc(s.sem("idx_product"), s.tick("idx_product"))

    def turn_rows(s, src, says):
        e = s.p.eng
        for k in range(KT):
            last = e.transpose(TURN[:, k * P:(k + 1) * P], t[src][:, k * P:(k + 1) * P], ident)
        last.then_inc(s.sem(says), s.tick(says))

    def turn_x(s, b):
        s.p.eng.wait_ge(s.sem("x_gathered"), s.at("x_gathered", 16 * (b + 1)))
        s.p.eng.wait_ge(s.sem("idx_ready"), s.at("idx_ready", b + 1))
        turn_rows(s, "xrow", "x_turned")

    def gate_product(s, b, between=None):
        for n in ("xt_hi", "xt_lo", "sel_gu"):
            s.p.eng.wait_ge(s.sem(n), s.at(n, b + 1))
        s.p.eng.wait_ge(s.sem("g_read"), s.at("g_read", b))
        bias(s.p.eng, GATE, "sel_gu", 0)
        for c in range(4):
            multiply(s, c, GATE, "xt")
            if between and c == 1:
                between()

    def up_product(s, b):
        s.p.eng.wait_ge(s.sem("u_read"), s.at("u_read", b))
        bias(s.p.eng, UP, "sel_gu", 1)
        for c in range(4):
            multiply(s, c, UP, "xt")

    def down_product(s, b):
        for n in ("ht_hi", "ht_lo", "sel_d"):
            s.p.eng.wait_ge(s.sem(n), s.at(n, b + 1))
        s.p.eng.wait_ge(s.sem("y_ready"), s.at("y_ready", b))
        bias(s.p.eng, DOWN, "sel_d", 2)
        for c in range(4):
            multiply(s, c, DOWN, "ht")

    def tensor_experts(e):
        p = Port(e, sem)
        e.wait_ge(sem("router_in"), p.next("router_in", 32))
        def turn_tile(i, n):
            e.wait_ge(sem("rows_normed"), p.next("rows_normed"))
            pair = (GATE, UP)[i % 2]
            for k in range(KT):
                last = e.transpose(pair[:, k * P:k * P + n], t["x1"][0:n, i, k * P:(k + 1) * P], ident[0:n, 0:n])
            last.then_inc(sem("x1_turned"), p.tick("x1_turned"))

        turn_tile(*rows[0])
        for i, n in rows:
            if i + 1 < TT:
                if i:
                    e.wait_ge(sem("x1t_ready"), p.at("x1t_ready", i))
                turn_tile(*rows[i + 1])
            e.wait_ge(sem("x1t_ready"), p.at("x1t_ready", i + 1))
            for k in range(KT):
                last = e.matmul(DOWN[0:n, i * NE:(i + 1) * NE], t["x1t"][:, i % 2, k, 0:n], t["rw"][:, k, :], start=k == 0, stop=k == KT - 1)
            last.then_inc(sem("logits_tile"), p.tick("logits_tile"))
        e.wait_ge(sem("chosen_ready"), p.next("chosen_ready"))
        e.wait_ge(sem("pool_constants"), p.next("pool_constants"))
        for i in range(TT):
            for j in range(i + 1):
                last = e.matmul(DOWN[:, 512 + i * NE:512 + (i + 1) * NE], t["before_b" if j == i else "ones_b"][:, :], t["mb"][:, j, :],
                                start=j == 0, stop=j == i)
        for j in range(TT):
            last = e.matmul(TURN[:, 0:NE], t["ones_b"][:, :], t["mb"][:, j, :], start=j == 0, stop=j == TT - 1)
        last.then_inc(sem("rank_product"), p.tick("rank_product"))
        s = Stream(p, "m_")
        find(s, 0)
        turn_x(s, 0)
        e.wait_ge(sem("bias_part"), p.next("bias_part", 2))

        def turn(b):
            gate_product(s, b, lambda: find(s, b + 1))
            if b:
                s.p.eng.wait_ge(s.sem("h_ready"), s.at("h_ready", b))
                s.p.eng.wait_ge(s.sem("idx_ready"), s.at("idx_ready", b + 2))
                turn_rows(s, "um", "h_turned")
            up_product(s, b)
            if b:
                s.p.eng.wait_ge(s.sem("ht_hi"), s.at("ht_hi", b))
                s.p.eng.wait_ge(s.sem("ht_lo"), s.at("ht_lo", b))
            turn_x(s, b + 1)
            if b:
                down_product(s, b - 1)

        turn(0)
        turn(1)
        with blocks(p, "m_", NE - 2):
            turn(2)
        s.n = s.start(NE)
        for n in ("h_ready", "xt_hi", "xt_lo"):
            s.p.eng.wait_ge(s.sem(n), s.at(n, NE if n == "h_ready" else NE + 1))
        turn_rows(s, "um", "h_turned")
        down_product(s, NE - 1)

    def tensor_extra(e):
        p = Port(e, sem, BASE)
        n = e.value_load(t["ints"][0:1, 0:1], min_val=0, max_val=NB_EXTRA)
        with e.If(n > 0):
            s = Stream(p, "o_")
            with blocks(p, "o_", n):
                s.p.eng.wait_ge(s.sem("ht_hi"), s.at("ht_hi", 0))
                s.p.eng.wait_ge(s.sem("ht_lo"), s.at("ht_lo", 0))
                find(s, 0)
                turn_x(s, 0)
                gate_product(s, 0)
                up_product(s, 0)
                s.p.eng.wait_ge(s.sem("h_ready"), s.at("h_ready", 1))
                s.p.eng.wait_ge(s.sem("xt_hi"), s.at("xt_hi", 1))
                s.p.eng.wait_ge(s.sem("xt_lo"), s.at("xt_lo", 1))
                turn_rows(s, "um", "h_turned")
                down_product(s, 0)

    def gather_rows(s, b):
        s.p.eng.wait_ge(s.sem("idx_ready"), s.at("idx_ready", b + 1))
        s.p.eng.wait_ge(s.sem("x_turned"), s.at("x_turned", b))
        s.p.eng.wait_ge(s.sem("passed"), s.at("passed", b))
        s.p.eng.tensor_tensor(t["mark"][:, 1:2], t["mark"][:, 0:1], t["mark"][:, 0:1], ALU.add).then_inc(s.sem("passed"), s.tick("passed"))
        s.p.eng.indirect_dma_start(
            out=t["xrow"][:, :], out_offset=None, in_=x1d[:, :], in_offset=bass.IndirectOffsetOnAxis(ap=t["idx"][:, 0:1], axis=0)).then_inc(sem(s.pre + "x_gathered"), s.p.tick(s.pre + "x_gathered", 16))

    def gpsimd_experts(e):
        p = Port(e, sem)

        e.dma_start(t["ln_g"][:, :], a["ln1_g"].to_broadcast([P, D])).then_inc(sem("ln_in"), p.tick("ln_in", 16))
        e.dma_start(t["ln_b"][:, :], a["ln1_b"].to_broadcast([P, D])).then_inc(sem("ln_in"), p.tick("ln_in", 16))
        e.dma_start(t["rw"][:, :, :], a["router_w"][0].rearrange("(k p) n -> p k n", p=P)).then_inc(sem("router_in"), p.tick("router_in", 16))
        e.dma_start(t["rb"][:, :], a["router_b"].to_broadcast([P, NE])).then_inc(sem("router_in"), p.tick("router_in", 16))
        e.iota(t["iota_i"][:, :], pattern=[[1, P]], base=0, channel_multiplier=0).then_inc(sem("pool"), p.tick("pool"))
        e.iota(t["tid_i"][:, :], pattern=[[0, 2 * TT]], base=0, channel_multiplier=1).then_inc(sem("pool"), p.tick("pool"))
        e.memset(t["eye"][:, :], 0.0).then_inc(sem("pool"), p.tick("pool"))
        e.memset(t["mark"][:, :], 0.0).then_inc(sem("pool"), p.tick("pool"))
        e.memset(t["ones_b"][:, :], 1.0).then_inc(sem("pool"), p.tick("pool"))
        e.tensor_copy(t["before_b"][:, :], t["mask01"][:, :]).then_inc(sem("pool"), p.tick("pool"))
        e.wait_ge(sem("pool"), p.now("pool"))
        e.tensor_copy(t["iota_c"][:, :], t["iota_i"][:, :]).then_inc(sem("pool"), p.tick("pool"))
        e.tensor_copy(t["tid"][:, :, :].rearrange("p i o -> p (i o)"), t["tid_i"][:, :]).then_inc(sem("pool"), p.tick("pool"))
        e.wait_ge(sem("pool"), p.now("pool"))
        for i in range(TT):
            e.memset(t["tid"][:, i, 1:2], float(P * i)).then_inc(sem("pool"), p.tick("pool"))
        for g in range(3):
            e.affine_select(out=t["eye"][:, :], in_=t["eye"][:, :], pattern=[[-1, NE + 1]], compare_op=ALU.not_equal, fill=1.0,
                               base=-g * NE, channel_multiplier=1).then_inc(sem("pool"), p.tick("pool"))
            e.wait_ge(sem("pool"), p.now("pool"))
        e.nop().then_inc(sem("pool_constants"), p.tick("pool_constants"))
        for r in (slice(0, 96), slice(64, 96)):
            e.wait_ge(sem("bias_rounded"), p.next("bias_rounded"))
            e.tensor_tensor(t["b_raw"][r, :], t["b_raw"][r, :], t["bb"][r, :], ALU.subtract).then_inc(sem("bias_rest"), p.tick("bias_rest"))
            e.wait_ge(sem("bias_rest"), p.now("bias_rest"))
        e.wait_ge(sem("bias_part"), p.next("bias_part", 2))
        e.wait_ge(sem("rows_moved"), p.at("rows_moved", 64 + 16 * TT))
        s = Stream(p, "m_")
        gather_rows(s, 0)
        e.wait_ge(sem("x1_turned"), p.next("x1_turned", TT))
        residual = iter(rows)

        def scale_residual():
            i, n = next(residual)
            e.tensor_scalar(t["x1"][0:n, i, :], t["x1"][0:n, i, :], ALPHA, None, ALU.mult).then_inc(sem("pool"), p.tick("pool"))

        def turn(b):
            s.n += 3
            remainder(s)
            gather_rows(s, b + 1)
            for c in range(2 if b else 1):
                if b < 2:
                    scale_residual()
                s.n += 3
                remainder(s)
            if b < 2:
                scale_residual()

        turn(0)
        turn(1)
        with blocks(p, "m_", NE - 2):
            turn(2)
        s.n = s.start(NE) + 3
        remainder(s)

    def gpsimd_extra(e):
        p = Port(e, sem, BASE)
        n = e.value_load(t["ints"][0:1, 0:1], min_val=0, max_val=NB_EXTRA)
        with e.If(n > 0):
            s = Stream(p, "o_")
            with blocks(p, "o_", n):
                gather_rows(s, 0)

    LN2_BASE = {"variance": 1, "deviation": 1, "rows_normed": TT, "rows_moved": 64 + 16 * TT, "ln_in": 32}

    def gpsimd_combine(e):
        p = Port(e, sem, LN2_BASE)
        e.dma_start(t["ln_g"][:, :], a["ln2_g"].to_broadcast([P, D])).then_inc(sem("ln_in"), p.tick("ln_in", 16))
        e.dma_start(t["ln_b"][:, :], a["ln2_b"].to_broadcast([P, D])).then_inc(sem("ln_in"), p.tick("ln_in", 16))
        for i, n in rows:
            if i >= 2:
                e.wait_ge(sem("summed"), p.next("summed"))
            for k in range(TOPK):
                e.indirect_dma_start(
                    out=t["yg"][0:n, i % 2, k, :], out_offset=None, in_=yd[:, :],
                    in_offset=bass.IndirectOffsetOnAxis(ap=t["posu"][0:n, i * TOPK + k:i * TOPK + k + 1], axis=0)).then_inc(sem(f"y_gathered{i % 2}"), p.tick(f"y_gathered{i % 2}", 16))

    def vector_combine(e):
        p = Port(e, sem, LN2_BASE)

        def normed(i, n):
            x = t["x1"][0:n, i, :]
            e.wait_ge(sem("deviation"), p.next("deviation", 3))
            e.tensor_tensor(x, x, t["ln_g"][0:n, :], ALU.mult).then_inc(sem("dve2"), p.tick("dve2"))
            e.wait_ge(sem("dve2"), p.now("dve2"))
            e.tensor_tensor(x, x, t["ln_b"][0:n, :], ALU.add).then_inc(sem("rows_normed"), p.tick("rows_normed"))

        e.wait_ge(sem("ln_in"), p.at("ln_in", 32))
        for i, n in rows:
            x = t["x1"][0:n, i, :]
            e.wait_ge(sem(f"y_gathered{i % 2}"), p.next(f"y_gathered{i % 2}", 64))
            for k in range(TOPK):
                e.scalar_tensor_tensor(
                    out=x, in0=t["yg"][0:n, i % 2, k, :], scalar=t["wk"][0:n, i, k:k + 1], in1=x, op0=ALU.mult, op1=ALU.add).then_inc(sem("dve2" if k < 3 else "summed"), p.tick("dve2" if k < 3 else "summed"))
                e.wait_ge(sem("dve2" if k < 3 else "summed"), p.now("dve2" if k < 3 else "summed"))
            for h in range(2):
                e.bn_stats(t["stats"][0:n, i, h, :], x[:, h * 512:(h + 1) * 512]).then_inc(sem("dve2"), p.tick("dve2"))
            e.wait_ge(sem("dve2"), p.now("dve2"))
            e.bn_aggr(t["mv"][0:n, i, :], t["stats"][0:n, i, 0:2, :]).then_inc(sem("dve2"), p.tick("dve2"))
            e.wait_ge(sem("dve2"), p.now("dve2"))
            r = t["rs"][0:n, i:i + 1]
            e.tensor_scalar(r, t["mv"][0:n, i, 1:2], EPS, None, ALU.add).then_inc(sem("dve2"), p.tick("dve2"))
            m = t["mv"][0:n, i, 0:1]
            e.tensor_scalar(m, m, -1.0, None, ALU.mult).then_inc(sem("dve2"), p.tick("dve2"))
            e.wait_ge(sem("dve2"), p.now("dve2"))
            e.reciprocal(r, r).then_inc(sem("variance"), p.tick("variance"))
            if i:
                normed(*rows[i - 1])
        normed(*rows[TT - 1])

    def scalar_combine(e):
        p = Port(e, sem, LN2_BASE)
        for i, n in rows:
            e.wait_ge(sem("variance"), p.next("variance"))
            r = t["rs"][0:n, i:i + 1]
            e.activation(r, r, ACT.Sqrt).then_inc(sem("deviation"), p.tick("deviation"))
            e.wait_ge(sem("deviation"), p.now("deviation"))
            m = t["mv"][0:n, i, 0:1]
            e.activation(m, m, ACT.Copy, scale=r).then_inc(sem("deviation"), p.tick("deviation"))
            e.wait_ge(sem("deviation"), p.now("deviation"))
            x = t["x1"][0:n, i, :]
            e.activation(x, x, ACT.Identity, scale=r, bias=m).then_inc(sem("deviation"), p.tick("deviation"))

    def sync_combine(e):
        p = Port(e, sem, LN2_BASE)
        for i, n in rows:
            e.wait_ge(sem("rows_normed"), p.next("rows_normed"))
            dst = out["y_prompt"][0, i * P:(i + 1) * P, :] if i < TT - 1 else out["y_sample"][:, 0, :]
            e.dma_start(dst, t["x1"][0:n, i, :]).then_inc(sem("rows_moved"), p.tick("rows_moved", 16))
        e.wait_ge(sem("rows_moved"), p.now("rows_moved"))

    with nc.Block() as block:
        @block.sync
        def _(e):
            sync_program(e)

        @block.scalar
        def _(e):
            scalar_dense(e)

        @block.vector
        def _(e):
            vector_dense(e)

        @block.tensor
        def _(e):
            tensor_dense(e)

        @block.gpsimd
        def _(e):
            gpsimd_dense(e)

    with nc.Block() as block:
        @block.sync
        def _(e):
            sync_experts(e)

        @block.scalar
        def _(e):
            scalar_experts(e)

        @block.vector
        def _(e):
            vector_experts(e)

        @block.tensor
        def _(e):
            tensor_experts(e)

        @block.gpsimd
        def _(e):
            gpsimd_experts(e)

    with nc.Block() as block:
        @block.sync
        def _(e):
            sync_extra(e)

        @block.scalar
        def _(e):
            scalar_extra(e)

        @block.vector
        def _(e):
            vector_extra(e)

        @block.tensor
        def _(e):
            tensor_extra(e)

        @block.gpsimd
        def _(e):
            gpsimd_extra(e)

    with nc.Block() as block:
        @block.sync
        def _(e):
            sync_combine(e)

        @block.scalar
        def _(e):
            scalar_combine(e)

        @block.vector
        def _(e):
            vector_combine(e)

        @block.gpsimd
        def _(e):
            gpsimd_combine(e)


_INS = ["x_prompt", "x_sample", "cache_k", "cache_v", "state_lru_h", "state_lru_conv", "state_conf_conv", "page_table",
        "w_in", "b_merge", "sb_bias", "lru_conv_w", "lru_conv_b", "lru_wa", "lru_ba", "lru_wx", "lru_bx", "lru_lambda",
        "conf_conv_w", "conf_conv_b", "conf_ln_g", "conf_ln_b", "w_branch", "w_out", "ln1_g", "ln1_b", "router_w",
        "router_b", "moe_w_gate", "moe_b_gate", "moe_w_up", "moe_b_up", "moe_w_down", "moe_b_down", "ln2_g", "ln2_b"]
_OUTS = {"y_prompt": (1, SEQ, D), "y_sample": (DEC, 1, D), "k_prompt": (1, 1, SEQ, HA, DA), "v_prompt": (1, 1, SEQ, HA, DA),
         "k_sample": (1, DEC, 1, HA, DA), "v_sample": (1, DEC, 1, HA, DA), "lru_h_prompt": (1, 1, W), "lru_h_sample": (1, DEC, W),
         "lru_conv_prompt": (1, 1, CB - 1, W), "lru_conv_sample": (1, DEC, CB - 1, W),
         "conf_conv_prompt": (1, 1, CC - 1, W), "conf_conv_sample": (1, DEC, CC - 1, W)}


def kernel(**inputs):
    import numpy as _np
    import concourse.bacc as _bacc
    from concourse.bass_utils import run_bass_kernel_spmd as _run

    nc = _bacc.Bacc("TRN2", target_bir_lowering=False, num_devices=1)
    arrays, a, out = {}, {}, {}
    for name in _INS:
        x = _np.ascontiguousarray(inputs[name])
        arrays[f"in_{name}_dram"] = x
        a[name] = nc.dram_tensor(f"in_{name}_dram", x.shape, mybir.dt.from_np(x.dtype), kind="ExternalInput").ap()
    for i, (name, shape) in enumerate(_OUTS.items()):
        out[name] = nc.dram_tensor(f"out_{i}_dram", shape, F32, kind="ExternalOutput").ap()
    build(nc, a, out)
    r = _run(nc, [arrays], core_ids=[0])
    return tuple(r.results[0][f"out_{i}_dram"] for i in range(len(_OUTS)))
```
